# Optimizing a Trainium2 kernel written in Bass

```python
import math
import jax, jax.numpy as jnp
from jax import lax
import numpy as np

D_MODEL = 1024
BATCH = 1
SEQ = 512
DEPTH = 1

CHUNK = 64
N_MEM = 256
EPS = 1e-6
NEG_INF = -1e30
N_NORMS = 6

BRANCH_DIM = D_MODEL // 2
N_BRANCH = 3

HEAD_DIM = 64
A_Q_HEADS = BRANCH_DIM // HEAD_DIM
A_KV_HEADS = 2
A_GROUP = A_Q_HEADS // A_KV_HEADS
A_Q_DIM = A_Q_HEADS * HEAD_DIM
A_KV_DIM = A_KV_HEADS * HEAD_DIM
WINDOW = 128
WINDOW_CHUNKS = WINDOW // CHUNK
ATT_BLOCK = 128

SGU_CHUNK = 128
SGU_GROUPS = 4
SGU_DIM = BRANCH_DIM
SGU_GROUP_DIM = SGU_DIM // SGU_GROUPS

POOL_WINDOWS = (2, 4, 8, 16)
POOL_GROUPS = 4
POOL_DIM = BRANCH_DIM
POOL_GROUP_DIM = POOL_DIM // POOL_GROUPS

IN_SIZES = (A_Q_DIM, A_KV_DIM, A_KV_DIM, SGU_DIM, SGU_DIM, POOL_DIM, N_BRANCH * D_MODEL)
IN_DIM = A_Q_DIM + 2 * A_KV_DIM + 2 * SGU_DIM + POOL_DIM + N_BRANCH * D_MODEL

MEM_HEADS = 4
MEM_HEAD_DIM = 128
MEM_DIM = MEM_HEADS * MEM_HEAD_DIM

D_FF = 4 * D_MODEL


def rmsnorm(x, g):
    xf = x.astype(jnp.float32)
    y = xf * lax.rsqrt(jnp.mean(xf * xf, axis=-1, keepdims=True) + EPS)
    return (y * g.astype(jnp.float32)).astype(x.dtype)

def split_columns(proj):
    parts, start = [], 0
    for size in IN_SIZES:
        parts.append(proj[..., start:start + size])
        start += size
    return parts

def window_sink_attention(q, k, v, sinks):
    B, S, _ = q.shape
    nb = S // ATT_BLOCK
    qb = q.reshape(B, nb, ATT_BLOCK, A_KV_HEADS, A_GROUP, HEAD_DIM)

    def band(t):
        t = t.reshape(B, S, A_KV_HEADS, HEAD_DIM)
        t = jnp.pad(t, ((0, 0), (ATT_BLOCK, 0), (0, 0), (0, 0)))
        t = t.reshape(B, nb + 1, ATT_BLOCK, A_KV_HEADS, HEAD_DIM)
        return jnp.concatenate([t[:, :-1], t[:, 1:]], axis=2)

    kb, vb = band(k), band(v)
    s = jnp.einsum('bnqhgd,bnkhd->bnhgqk', qb, kb).astype(jnp.float32) * (1.0 / math.sqrt(HEAD_DIM))

    blk = jnp.arange(nb)[:, None, None]
    qpos = blk * ATT_BLOCK + jnp.arange(ATT_BLOCK)[None, :, None]
    kpos = (blk - 1) * ATT_BLOCK + jnp.arange(2 * ATT_BLOCK)[None, None, :]
    qc, kc = qpos // CHUNK, kpos // CHUNK
    valid = (kpos >= 0) & (kc <= qc) & (kc >= qc - WINDOW_CHUNKS)
    s = jnp.where(valid[None, :, None, None], s, NEG_INF)

    sink = sinks.astype(jnp.float32).reshape(A_KV_HEADS, A_GROUP)[None, None, :, :, None, None]
    m = jnp.maximum(jnp.max(s, axis=-1, keepdims=True), sink)
    p = jnp.exp(s - m)
    p = p / (jnp.sum(p, axis=-1, keepdims=True) + jnp.exp(sink - m))
    o = jnp.einsum('bnhgqk,bnkhd->bnqhgd', p.astype(v.dtype), vb)
    return o.reshape(B, S, A_Q_DIM)

def spatial_gating(u, v, g_sgu, w_s, b_s):
    B, S, _ = u.shape
    nc = S // SGU_CHUNK
    u = jax.nn.gelu(u)
    v = rmsnorm(jax.nn.gelu(v), g_sgu)
    vb = v.reshape(B, nc, SGU_CHUNK, SGU_GROUPS, SGU_GROUP_DIM)
    pc = jnp.arange(SGU_CHUNK) // CHUNK
    mask = pc[None, :] <= pc[:, None]
    w = jnp.where(mask[None], w_s, 0.0).astype(v.dtype)
    sp = jnp.einsum('gij,bnjgc->bnigc', w, vb) + b_s.T[:, :, None].astype(v.dtype)
    return u * sp.reshape(B, S, SGU_DIM)

def multiscale_pool(c, w_pool, pool_scale):
    B, S, _ = c.shape
    cs = jnp.cumsum(c.astype(jnp.float32), axis=1)
    t = jnp.arange(S)
    outs = []
    for gi, w in enumerate(POOL_WINDOWS):
        cg = cs[..., gi * POOL_GROUP_DIM:(gi + 1) * POOL_GROUP_DIM]
        lag = jnp.pad(cg, ((0, 0), (w, 0), (0, 0)))[:, :S]
        cnt = jnp.minimum(t + 1, w).astype(jnp.float32)[None, :, None]
        outs.append((cg - lag) / cnt)
    pooled = jnp.concatenate(outs, axis=-1).astype(c.dtype) - c
    pooled = pooled.reshape(B, S, POOL_GROUPS, POOL_GROUP_DIM)
    mixed = jnp.einsum('bsgc,gcd->bsgd', pooled, w_pool).reshape(B, S, POOL_DIM)
    return mixed * pool_scale

def memory_attention(h, mem_n, w_q, w_kv, w_o):
    B, S, _ = h.shape
    q = (h @ w_q).reshape(B, S, MEM_HEADS, MEM_HEAD_DIM)
    kv = mem_n @ w_kv
    k = kv[..., :MEM_DIM].reshape(B, N_MEM, MEM_HEADS, MEM_HEAD_DIM)
    v = kv[..., MEM_DIM:].reshape(B, N_MEM, MEM_HEADS, MEM_HEAD_DIM)
    s = jnp.einsum('bshd,bmhd->bhsm', q, k).astype(jnp.float32) * (1.0 / math.sqrt(MEM_HEAD_DIM))
    p = jax.nn.softmax(s, axis=-1).astype(h.dtype)
    o = jnp.einsum('bhsm,bmhd->bshd', p, v).reshape(B, S, MEM_DIM)
    return o @ w_o

def first_inputs(seed: int = 0) -> dict:
    key = jax.random.key(seed)
    ks = jax.random.split(key, 20)
    f32 = jnp.float32

    def dense(k, shape, fan_in):
        return jax.random.normal(k, shape, f32) * (fan_in ** -0.5)

    return {
        "x": jax.random.normal(ks[0], (BATCH, SEQ, D_MODEL), f32),
        "mem": jax.random.normal(ks[1], (BATCH, N_MEM, D_MODEL), f32),
        "g_norm": 1.0 + 0.1 * jax.random.normal(ks[2], (DEPTH, N_NORMS, D_MODEL), f32),
        "g_mem": 1.0 + 0.1 * jax.random.normal(ks[3], (DEPTH, D_MODEL), f32),
        "w_in": dense(ks[4], (DEPTH, D_MODEL, IN_DIM), D_MODEL),
        "attn_sinks": 0.5 * jax.random.normal(ks[5], (DEPTH, A_Q_HEADS), f32),
        "w_spatial": dense(ks[6], (DEPTH, SGU_GROUPS, SGU_CHUNK, SGU_CHUNK), SGU_CHUNK),
        "b_spatial": 1.0 + 0.1 * jax.random.normal(ks[7], (DEPTH, SGU_GROUPS, SGU_CHUNK), f32),
        "g_sgu": 1.0 + 0.1 * jax.random.normal(ks[8], (DEPTH, SGU_DIM), f32),
        "w_pool": dense(ks[9], (DEPTH, POOL_GROUPS, POOL_GROUP_DIM, POOL_GROUP_DIM), POOL_GROUP_DIM),
        "pool_scale": 1.0 + 0.1 * jax.random.normal(ks[10], (DEPTH, POOL_DIM), f32),
        "w_branch": dense(ks[11], (DEPTH, N_BRANCH, BRANCH_DIM, D_MODEL), BRANCH_DIM),
        "w_out": dense(ks[12], (DEPTH, D_MODEL, D_MODEL), D_MODEL),
        "w_q_mem": dense(ks[13], (DEPTH, D_MODEL, MEM_DIM), D_MODEL),
        "w_kv_mem": dense(ks[14], (DEPTH, D_MODEL, 2 * MEM_DIM), D_MODEL),
        "w_o_mem": dense(ks[15], (DEPTH, MEM_DIM, D_MODEL), MEM_DIM),
        "w_up": dense(ks[16], (DEPTH, D_MODEL, D_FF), D_MODEL),
        "w_down": dense(ks[17], (DEPTH, D_FF, D_MODEL), D_FF),
    }

def first_block(x, mem, g_norm, g_mem, w_in, attn_sinks, w_spatial, b_spatial, g_sgu,
              w_pool, pool_scale, w_branch, w_out, w_q_mem, w_kv_mem, w_o_mem, w_up, w_down):
    B, S, _ = x.shape
    for l in range(DEPTH):
        h = rmsnorm(x, g_norm[l, 0])
        q, k, v, su, sv, pc, gate = split_columns(h @ w_in[l])
        ya = window_sink_attention(q, k, v, attn_sinks[l])
        yb = spatial_gating(su, sv, g_sgu[l], w_spatial[l], b_spatial[l])
        yc = multiscale_pool(pc, w_pool[l], pool_scale[l])
        branches = jnp.stack([ya, yb, yc], axis=2)
        proj = jnp.einsum('bsnc,ncd->bsnd', branches, w_branch[l])
        gates = jax.nn.sigmoid(gate.reshape(B, S, N_BRANCH, D_MODEL))
        merged = jnp.sum(gates * proj, axis=2)
        x = x + rmsnorm(merged @ w_out[l], g_norm[l, 1])
        hm = rmsnorm(x, g_norm[l, 2])
        mem_n = rmsnorm(mem, g_mem[l])
        ym = memory_attention(hm, mem_n, w_q_mem[l], w_kv_mem[l], w_o_mem[l])
        x = x + rmsnorm(ym, g_norm[l, 3])
        hf = rmsnorm(x, g_norm[l, 4])
        yf = jnp.square(jax.nn.relu(hf @ w_up[l])) @ w_down[l]
        x = x + rmsnorm(yf, g_norm[l, 5])
    return x


MLA_HEADS = 8
MLA_Q_RANK = 384
MLA_KV_RANK = 256
MLA_NOPE_DIM = 64
MLA_ROPE_DIM = 32
MLA_V_DIM = 64
MLA_QK_DIM = MLA_NOPE_DIM + MLA_ROPE_DIM
FOX_HEADS = 8
FOX_HEAD_DIM = 64
FOX_WIDTH = FOX_HEADS * FOX_HEAD_DIM
MIX_WIDTH = MLA_HEADS * MLA_V_DIM + FOX_WIDTH
ROPE_THETA = 10000.0
BLOCK_Q = 128
IN_SPLITS = (MLA_Q_RANK, MLA_KV_RANK, MLA_ROPE_DIM, FOX_WIDTH, FOX_WIDTH, FOX_WIDTH, FOX_HEADS)
IN_WIDTH = sum(IN_SPLITS)
PEER_HEADS = 8
N_KEYS = 128
N_EXPERTS = N_KEYS * N_KEYS
PEER_QDIM = 256
PEER_HALF = PEER_QDIM // 2
PEER_TOPK = 16
PEER_CHUNK = 64


def _rms_norm(x, g):
    xf = x.astype(jnp.float32)
    y = xf * lax.rsqrt(jnp.mean(xf * xf, axis=-1, keepdims=True) + EPS)
    return (y * g.astype(jnp.float32)).astype(x.dtype)

def _modulate(x, g, shift, scale):
    return _rms_norm(x, g) * (1.0 + scale) + shift

def _rope(x, ang):
    half = x.shape[-1] // 2
    x1, x2 = x[..., :half], x[..., half:]
    cos = jnp.cos(ang).astype(x.dtype)
    sin = jnp.sin(ang).astype(x.dtype)
    return jnp.concatenate([x1 * cos - x2 * sin, x2 * cos + x1 * sin], axis=-1)

def _causal_block_attention(q, k, v, scale, fcum=None):
    b, h, s, dk = q.shape
    dv = v.shape[-1]
    nblk = s // BLOCK_Q
    qb = q.reshape(b, h, nblk, BLOCK_Q, dk).transpose(2, 0, 1, 3, 4)
    kf = k.astype(jnp.float32)
    vf = v.astype(jnp.float32)
    key_pos = jnp.arange(s)
    blk_ids = jnp.arange(nblk)

    def scores(q_i):
        return jnp.einsum("bhqd,bhkd->bhqk", q_i.astype(jnp.float32), kf) * scale

    def finish(i, sc):
        q_pos = i * BLOCK_Q + jnp.arange(BLOCK_Q)
        sc = jnp.where(key_pos[None, :] <= q_pos[:, None], sc, -jnp.inf)
        p = jax.nn.softmax(sc, axis=-1)
        return jnp.einsum("bhqk,bhkd->bhqd", p, vf)

    if fcum is None:
        out = lax.map(lambda a: finish(a[0], scores(a[1])), (blk_ids, qb))
    else:
        fb = fcum.reshape(b, h, nblk, BLOCK_Q).transpose(2, 0, 1, 3)

        def blk(a):
            i, q_i, f_i = a
            sc = scores(q_i) + f_i[..., None] - fcum[:, :, None, :]
            return finish(i, sc)

        out = lax.map(blk, (blk_ids, qb, fb))
    return out.transpose(1, 2, 0, 3, 4).reshape(b, h, s, dv).astype(v.dtype)

def _peer(h, w_pq, sub_keys, peer_u, peer_v):
    b, s, d = h.shape
    qp = (h @ w_pq).astype(jnp.float32).reshape(b, s, PEER_HEADS, 2, PEER_HALF)
    sc = jnp.einsum("bshpd,hpnd->bshpn", qp, sub_keys.astype(jnp.float32))
    s1, i1 = lax.top_k(sc[..., 0, :], PEER_TOPK)
    s2, i2 = lax.top_k(sc[..., 1, :], PEER_TOPK)
    cand = (s1[..., :, None] + s2[..., None, :]).reshape(b, s, PEER_HEADS, PEER_TOPK * PEER_TOPK)
    top_s, top_c = lax.top_k(cand, PEER_TOPK)
    e1 = jnp.take_along_axis(i1, top_c // PEER_TOPK, axis=-1)
    e2 = jnp.take_along_axis(i2, top_c % PEER_TOPK, axis=-1)
    expert = e1 * N_KEYS + e2
    gate = jax.nn.softmax(top_s, axis=-1)
    nc = s // PEER_CHUNK

    def to_chunks(a):
        return a.reshape((b, nc, PEER_CHUNK) + a.shape[2:]).swapaxes(0, 1)

    def chunk(args):
        h_c, e_c, g_c = args
        u = jnp.take(peer_u, e_c, axis=0)
        a = jnp.einsum("bcd,bchkd->bchk", h_c.astype(jnp.float32), u.astype(jnp.float32))
        w = g_c * jax.nn.gelu(a)
        vv = jnp.take(peer_v, e_c, axis=0)
        return jnp.einsum("bchk,bchkd->bcd", w, vv.astype(jnp.float32))

    y = lax.map(chunk, (to_chunks(h), to_chunks(expert), to_chunks(gate)))
    return y.swapaxes(0, 1).reshape(b, s, d).astype(h.dtype)

def second_inputs(seed: int = 0) -> dict:
    key = jax.random.key(seed)
    ks = jax.random.split(key, 24)
    f32 = jnp.float32
    D = D_MODEL

    def nrm(k, shape, scale):
        return jax.random.normal(k, shape, f32) * scale

    def gain(k, n):
        return 1.0 + 0.02 * jax.random.normal(k, (n,), f32)

    x = jax.random.normal(ks[0], (BATCH, SEQ, D), f32)
    c = jax.random.normal(ks[1], (BATCH, D), f32)
    offset = jax.random.randint(ks[2], (BATCH, 1), 0, 1024, dtype=jnp.int32)
    positions = (offset + jnp.arange(SEQ, dtype=jnp.int32)[None, :]).astype(jnp.int32)
    return {
        "x": x,
        "c": c,
        "positions": positions,
        "w_ada": nrm(ks[3], (D, 6 * D), 0.5 * D ** -0.5),
        "b_ada": nrm(ks[4], (6 * D,), 0.01),
        "norm1_g": gain(ks[5], D),
        "w_in": nrm(ks[6], (D, IN_WIDTH), D ** -0.5),
        "mla_qa_g": gain(ks[7], MLA_Q_RANK),
        "mla_kva_g": gain(ks[8], MLA_KV_RANK),
        "w_uq": nrm(ks[9], (MLA_Q_RANK, MLA_HEADS * MLA_QK_DIM), MLA_Q_RANK ** -0.5),
        "w_ukv": nrm(ks[10], (MLA_KV_RANK, MLA_HEADS * (MLA_NOPE_DIM + MLA_V_DIM)), MLA_KV_RANK ** -0.5),
        "mla_q_g": gain(ks[11], MLA_QK_DIM),
        "mla_k_g": gain(ks[12], MLA_QK_DIM),
        "fox_q_g": gain(ks[13], FOX_HEAD_DIM),
        "fox_k_g": gain(ks[14], FOX_HEAD_DIM),
        "b_f": 2.0 + 0.5 * jax.random.normal(ks[15], (FOX_HEADS,), f32),
        "w_o": nrm(ks[16], (MIX_WIDTH, D), MIX_WIDTH ** -0.5),
        "norm2_g": gain(ks[17], D),
        "w_pq": nrm(ks[18], (D, PEER_HEADS * PEER_QDIM), D ** -0.5),
        "sub_keys": nrm(ks[19], (PEER_HEADS, 2, N_KEYS, PEER_HALF), PEER_HALF ** -0.5),
        "peer_u": nrm(ks[20], (N_EXPERTS, D), D ** -0.5),
        "peer_v": nrm(ks[21], (N_EXPERTS, D), PEER_HEADS ** -0.5),
    }

def second_block(x, c, positions, w_ada, b_ada, norm1_g, w_in, mla_qa_g, mla_kva_g, w_uq, w_ukv,
              mla_q_g, mla_k_g, fox_q_g, fox_k_g, b_f, w_o, norm2_g, w_pq, sub_keys, peer_u, peer_v):
    dt = x.dtype
    b, s, d = x.shape
    mod = jax.nn.silu(c.astype(jnp.float32)) @ w_ada.astype(jnp.float32) + b_ada.astype(jnp.float32)
    mod = mod.reshape(b, 6, 1, d).astype(dt)
    shift1, scale1, gate1 = mod[:, 0], mod[:, 1], mod[:, 2]
    shift2, scale2, gate2 = mod[:, 3], mod[:, 4], mod[:, 5]
    inv_freq = ROPE_THETA ** (-jnp.arange(0, MLA_ROPE_DIM, 2, dtype=jnp.float32) / MLA_ROPE_DIM)
    ang = (positions.astype(jnp.float32)[..., None] * inv_freq)[:, :, None, :]

    for _ in range(DEPTH):
        h = _modulate(x, norm1_g, shift1, scale1)
        proj = h @ w_in
        cq, ckv, kpe, fq, fk, fv, fl = jnp.split(proj, list(np.cumsum(IN_SPLITS)[:-1]), axis=-1)

        q_a = (_rms_norm(cq, mla_qa_g) @ w_uq).reshape(b, s, MLA_HEADS, MLA_QK_DIM)
        kv_a = (_rms_norm(ckv, mla_kva_g) @ w_ukv).reshape(b, s, MLA_HEADS, MLA_NOPE_DIM + MLA_V_DIM)
        k_nope, v_a = kv_a[..., :MLA_NOPE_DIM], kv_a[..., MLA_NOPE_DIM:]
        k_pe = jnp.broadcast_to(kpe[:, :, None, :], (b, s, MLA_HEADS, MLA_ROPE_DIM))
        k_a = jnp.concatenate([k_nope, k_pe], axis=-1)
        q_a = _rms_norm(q_a, mla_q_g)
        k_a = _rms_norm(k_a, mla_k_g)
        q_a = jnp.concatenate([q_a[..., :MLA_NOPE_DIM], _rope(q_a[..., MLA_NOPE_DIM:], ang)], axis=-1)
        k_a = jnp.concatenate([k_a[..., :MLA_NOPE_DIM], _rope(k_a[..., MLA_NOPE_DIM:], ang)], axis=-1)
        o_a = _causal_block_attention(q_a.transpose(0, 2, 1, 3), k_a.transpose(0, 2, 1, 3),
                                      v_a.transpose(0, 2, 1, 3), MLA_QK_DIM ** -0.5)

        q_b = _rms_norm(fq.reshape(b, s, FOX_HEADS, FOX_HEAD_DIM), fox_q_g)
        k_b = _rms_norm(fk.reshape(b, s, FOX_HEADS, FOX_HEAD_DIM), fox_k_g)
        v_b = fv.reshape(b, s, FOX_HEADS, FOX_HEAD_DIM)
        log_f = jax.nn.log_sigmoid(fl.astype(jnp.float32) + b_f.astype(jnp.float32))
        fcum = jnp.cumsum(log_f, axis=1).transpose(0, 2, 1)
        o_b = _causal_block_attention(q_b.transpose(0, 2, 1, 3), k_b.transpose(0, 2, 1, 3),
                                      v_b.transpose(0, 2, 1, 3), FOX_HEAD_DIM ** -0.5, fcum)

        o = jnp.concatenate([o_a, o_b], axis=1).transpose(0, 2, 1, 3).reshape(b, s, MIX_WIDTH)
        x = x + gate1 * (o @ w_o)

        h2 = _modulate(x, norm2_g, shift2, scale2)
        x = x + gate2 * _peer(h2, w_pq, sub_keys, peer_u, peer_v)
    return x


def setup_inputs(seed=0):
    out = dict(first_inputs(seed))
    for name, value in second_inputs(seed + 1).items():
        if name != "x":
            out[name + "_2"] = value
    return out


def reference(
    x, mem, g_norm, g_mem, w_in, attn_sinks, w_spatial, b_spatial, g_sgu, w_pool, pool_scale,
    w_branch, w_out, w_q_mem, w_kv_mem, w_o_mem, w_up, w_down, c_2, positions_2, w_ada_2,
    b_ada_2, norm1_g_2, w_in_2, mla_qa_g_2, mla_kva_g_2, w_uq_2, w_ukv_2, mla_q_g_2, mla_k_g_2,
    fox_q_g_2, fox_k_g_2, b_f_2, w_o_2, norm2_g_2, w_pq_2, sub_keys_2, peer_u_2, peer_v_2,
):
    x = first_block(
        x, mem, g_norm, g_mem, w_in, attn_sinks, w_spatial, b_spatial, g_sgu, w_pool,
        pool_scale, w_branch, w_out, w_q_mem, w_kv_mem, w_o_mem, w_up, w_down,
    )
    return second_block(
        x, c_2, positions_2, w_ada_2, b_ada_2, norm1_g_2, w_in_2, mla_qa_g_2, mla_kva_g_2,
        w_uq_2, w_ukv_2, mla_q_g_2, mla_k_g_2, fox_q_g_2, fox_k_g_2, b_f_2, w_o_2, norm2_g_2,
        w_pq_2, sub_keys_2, peer_u_2, peer_v_2,
    )


_drawn_inputs = setup_inputs


def setup_inputs(seed=0):
    import zlib

    import numpy as np

    out = dict(_drawn_inputs(seed))
    spreads = {}
    factors = {'attn_sinks': 8.0,
     'b_ada_2': 8.0,
     'norm1_g_2': 8.0,
     'mla_qa_g_2': 8.0,
     'mla_kva_g_2': 8.0,
     'w_uq_2': 4.902,
     'mla_q_g_2': 8.0,
     'mla_k_g_2': 8.0,
     'fox_q_g_2': 8.0,
     'fox_k_g_2': 8.0,
     'b_f_2': 4.184,
     'norm2_g_2': 8.0}
    for name, (base, spread) in spreads.items():
        noise = np.random.default_rng([zlib.crc32(name.encode()), seed]).standard_normal(out[name].shape)
        drawn = base * np.exp(spread * noise) if base else spread * noise
        out[name] = __import__('jax').numpy.asarray(drawn.astype(out[name].dtype))
    for name, factor in factors.items():
        out[name] = (out[name] * factor).astype(out[name].dtype)
    return out
```

```python
import math
from contextlib import ExitStack

import numpy as np
import concourse.bass as bass
from concourse import mybir

F32 = mybir.dt.float32
U32 = mybir.dt.uint32
I32 = mybir.dt.int32
ALU = mybir.AluOpType
ACT = mybir.ActivationFunctionType
AX_X = mybir.AxisListType.X
ds = bass.ds

P = 128
SEQ = 512
NT = SEQ // P
D = 1024
KB = D // P
N_MEM = 256
EPS = 1e-6
NEG = -1e30
FF_BLOCKS = 32
CH = 1024
RING = 4
TOPK = 16
HEADS = 8
N_KEYS = 128
QK = 96
ROPE_HALF = 16
POOL_PAD = 16
UG = 4
ROWS_PER_TILE = HEADS * TOPK
PER_HEAD = TOPK // UG
EARLY = 6

COLS = {}
_at = 0
for _name, _n in (("c", 8), ("g0", 8), ("g1", 8), ("g2", 8), ("g3", 8), ("g4", 8), ("g5", 8),
                  ("g_mem", 8), ("pool_scale", 4), ("qa_g", 3), ("kva_g", 2), ("norm1_g", 8)):
    COLS[_name] = slice(_at, _at + _n)
    _at += _n
N_COLS = _at
ROWS = {}
_at = 0
for _name, _n in (("sinks", 8), ("b_f", 8), ("mla_q_g", QK), ("mla_k_g", QK), ("fox_q_g", 64), ("fox_k_g", 64)):
    ROWS[_name] = slice(_at, _at + _n)
    _at += _n
N_ROWS = _at
CST = {"ident": slice(0, 128), "mask_band": slice(128, 384), "mask_diag": slice(384, 512),
       "iota16": slice(512, 528), "inv_freq": slice(528, 544)}
N_CST = 544

STREAM = (("v_attn", 1), ("q_attn", 4), ("k_attn", 1), ("kv_mem_k", 4), ("kv_mem_v", 4), ("sgu_v", 4), ("sgu_u", 4),
          ("pool_c", 4), ("gate0", 8), ("branch0", 4), ("gate1", 8), ("branch1", 4), ("gate2", 8), ("branch2", 4),
          ("out", 8), ("q_mem", 4), ("o_mem", 4), ("up", 32), ("down", 32),
          ("cq_ckv", 5), ("misc", 1), ("fox_q", 4), ("fox_k", 4), ("fox_v", 4), ("uq", 3), ("ukv", 2), ("o2", 8), ("pq", 16))
N_CHUNKS = sum(n for _, n in STREAM)
LIN_MOD_COLS = 27 + 8 + 48 + 8 + 4 + 8 + 32 + 8 + 1

MAGIC = 12582912.0
TWO_PI_A = 6.28125
TWO_PI_B = 0.0019350051879882812
TWO_PI_C = 2 * math.pi - TWO_PI_A - TWO_PI_B


class Steps:

    def __init__(self, eng, own):
        self.eng, self.own, self.count, self.loop = eng, own, {}, None

    def value(self, sem):
        n = self.count.get(sem.name, 0)
        if self.loop is not None and sem.name in self.loop[1]:
            reg, per, base = self.loop
            return reg * per[sem.name] + n
        return n

    def tell(self, ins, sem, by=1):
        self.count[sem.name] = self.count.get(sem.name, 0) + by
        ins.then_inc(sem, by)

    def __call__(self, ins, sem=None):
        sem = self.own if sem is None else sem
        self.tell(ins, sem)
        self.eng.wait_ge(sem, self.value(sem))

    def enter(self, reg, per):
        self.loop = (reg, {s.name: k for s, k in per}, dict(self.count))

    def leave(self, iterations):
        _, per, base = self.loop
        for name, k in per.items():
            assert self.count[name] - base.get(name, 0) == k, (name, self.count[name], base.get(name, 0), k)
            self.count[name] = base.get(name, 0) + k * iterations
        self.loop = None


def attention_plan():
    plan = {}
    u = g = 0
    for kind, heads in (("band", 8), ("mem", 4), ("mla", 8), ("fox", 8)):
        units = []
        for t in range(NT):
            for h in range(heads):
                if kind == "band":
                    blocks = [t - 1, t] if t else [0]
                elif kind == "mem":
                    blocks = [0, 1]
                else:
                    blocks = list(range(t + 1))
                units.append(dict(u=u, g=g, t=t, h=h, blocks=blocks, last=h == heads - 1))
                u += 1
            g += 1
        plan[kind] = dict(units=units, heads=heads, dv=512 // heads)
    return plan


def build(nc, T, out):
    plan = attention_plan()
    with ExitStack() as ctx:
        def sb(name, shape, dt=F32):
            return ctx.enter_context(nc.sbuf_tensor(name, shape, dt))

        def sem(name):
            return ctx.enter_context(nc.semaphore(name))

        main = sb("main", [P, 4 * 4096 + 20480])
        def region(lo, *shape):
            n = int(np.prod(shape))
            v = main[:, lo:lo + n]
            if len(shape) == 2:
                return v.rearrange("p (a b) -> p a b", a=shape[0])
            if len(shape) == 3:
                return v.rearrange("p (a b c) -> p a b c", a=shape[0], b=shape[1])
            return v
        X0, H0, Z0, S0, A0 = 0, 4096, 8192, 12288, 16384
        xT = region(X0, KB, SEQ)
        hT = region(H0, KB, SEQ)
        zT = region(Z0, KB, SEQ)
        sqT = region(S0, KB, SEQ)
        inv_cnt = region(Z0, 4, SEQ)
        g_sgu_row = region(Z0 + 2048, 512)
        b_sp_row = region(Z0 + 2560, 4, P)
        w_pool = region(Z0 + 3072, 4, P)
        w_spT = region(Z0 + 3584, 4, P)
        uT = region(A0, 4, SEQ)
        cT = region(A0 + 2048, 4, SEQ + POOL_PAD)
        yaT = region(A0 + 4160, 4, SEQ)
        kmT = region(A0 + 6208, 4, N_MEM)
        vm = region(A0 + 7232, 2, 512)
        q1T = region(A0 + 8256, 4, SEQ)
        k1T = region(A0 + 10304, SEQ)
        v1 = region(A0 + 10816, NT, P)
        vS = region(A0 + 11328, NT, 512)
        memT = region(A0 + 13376, KB, N_MEM)
        gates = region(A0 + 8256, KB, SEQ)
        merged = region(A0 + 12352, KB, SEQ)
        pool_a = region(A0 + 16448, SEQ + POOL_PAD)
        pool_b = region(A0 + 16976, SEQ + POOL_PAD)
        ycT = region(A0 + 17504, 4, SEQ)
        qmT = region(A0 + 8256, 4, SEQ)
        ymT = region(A0 + 10304, 4, SEQ)
        hid = region(A0, FF_BLOCKS, SEQ)
        probs = region(S0, 2, 512)
        probsT = region(S0 + 1024, 2, 512)
        o_tok = region(S0 + 2048, 2, 512)
        qT = region(A0, HEADS, SEQ)
        kT = region(A0 + 4096, HEADS, SEQ)
        k_tok = region(A0, NT, HEADS, QK)
        q_tok = region(H0, NT, HEADS, QK)
        cqT = region(A0 + 4096, 5, SEQ)
        fqT = region(A0 + 8192, 4, SEQ)
        fkT = region(A0 + 10240, 4, SEQ)
        f_row = region(A0 + 12288, HEADS, SEQ)
        v_mla = region(A0 + 16384, NT, 512)
        v_fox = region(A0 + 18432, NT, 512)
        fq_tok = region(Z0, NT, 512)
        fk_tok = region(Z0 + 2048, NT, 512)
        sq_tok = region(S0, NT, HEADS * QK)
        oT = region(H0, KB, SEQ)
        u_rows = region(A0, 2 * UG, D)
        v_rows = region(A0 + 8192, 2 * UG, D)
        x_tok = region(A0 + 16384, NT, D)
        h2_tok = region(S0, NT, D)
        h2T = region(Z0, KB, SEQ)
        qpT = region(X0, 2 * HEADS, SEQ)

        ring = sb("ring", [P, RING, CH])
        ada_ring = sb("ada_ring", [P, 2, CH])
        sub_keys = ada_ring[:, :, :].rearrange("p a b -> p (a b)").rearrange("p (k n) -> p k n", n=N_KEYS)
        mod = sb("mod", [P, 6, D])
        scores = [mod[:, 0:2, :].rearrange("p a b -> p (a b)"), ring[:, 0:2, :].rearrange("p a b -> p (a b)")]
        onehot = sb("onehot", [P, 2 * TOPK * TOPK])
        cols = sb("cols", [P, N_COLS])
        rows = sb("rows", [P, N_ROWS])
        cst = sb("cst", [P, N_CST])
        sel = mod[0:HEADS, 1, :]
        ones = sb("ones", [P, P])
        diag = sb("diag", [P, NT, P])
        eps = sb("eps", [P, 1])
        std = sb("std", [P, NT])
        rstd = sb("rstd", [P, NT])
        silu_c = sb("silu_c", [P, KB])
        c_now = sb("c_now", [P, 1])
        mod_cols = sb("mod_cols", [P, 2 * KB])
        mx = sb("mx", [P, 2, HEADS])
        neg_m = sb("neg_m", [P, 2, HEADS])
        row_sum = sb("row_sum", [P, 2, HEADS])
        sink_e = sb("sink_e", [P, 2, HEADS])
        ident = cst[:, CST["ident"]]
        cand = cst[:, CST["mask_band"]]
        small = sb("small", [P, 640])

        def sm(lo, n):
            return small[:, lo:lo + n]
        misc_tok = sm(0, 160).rearrange("p (t n) -> p t n", t=NT)
        fl_a = sm(160, 32)
        fl_b = sm(192, 32)
        pos_f = sm(224, 4)
        ang = sm(228, 64)
        turns = sm(292, 64)
        sin_t = sm(356, 64)
        cos_t = sm(420, 64)
        ss_tok = sm(484, 32)
        r_tok = sm(516, 32)
        fq_col = sm(548, 32).rearrange("p (t h) -> p t h", t=NT)
        pos_i = sb("pos_i", [P, NT], I32)
        f_cum = diag[0:HEADS, :, :].rearrange("p a b -> p (a b)")
        f_log = mod[0:HEADS, 0, 0:512]

        psum = [ctx.enter_context(nc.psum_tensor(f"bank{i}", [P, 512], F32)) for i in range(8)]

        names = ("consts_in cols_in rows_in x_in mem_in sgu_in ada_b_in pos_in sub_in sel_in gn2_in "
                 "w_used lin_ready lin_evacuated sq_ready sumsq_ready std_ready diag_ready rbc_ready h_ready mem_ready "
                 "ones_ready acc_zero sig_c x_ready silu_ready v_sq_ready vstd_ready vs_ready wsp_ready yb_ready pooled_ready "
                 "pads_zero merged_ready hid_ready ada_used mod_ready cqn_ready "
                 "s_ready neg_ready p_ready pt_ready pt_copied av_done o_normed ot_ready ot_copied sink_arg sink_exp "
                 "fl_arg fl_exp fl_ready f_cum_ready trig_arg trig_ready gain_ready tok_sq tok_ss tok_std tok_ready "
                 "h2_sq h2_std h2_ready x2_ready sc_ready sc_copied top_arg top_exp "
                 "u_used gl_ready w_ready dg_ready v_used y_ready y_added stored "
                 "pe_own act_own dve_own pool_own").split()
        S = {n: sem(n) for n in names}
        w_landed = [sem(f"w_landed{i}") for i in range(RING)]
        ada_landed = [sem(f"ada_landed{i}") for i in range(2)]
        u_landed = [sem(f"u_landed{i}") for i in range(2 * UG)]
        v_landed = [sem(f"v_landed{i}") for i in range(2 * UG)]
        idx = sb("idx", [P, NT, ROWS_PER_TILE], U32)
        gate_w = sb("gate_w", [P, 2, ROWS_PER_TILE])
        top_v = sb("top_v", [P, 2 * TOPK])
        top_i = sb("top_i", [P, 2 * TOPK], U32)
        top_if = sb("top_if", [P, 2 * TOPK])
        best_v = sb("best_v", [P, TOPK])
        best_i = sb("best_i", [P, TOPK], U32)
        best_hi = sb("best_hi", [P, 2 * TOPK], U32)
        best_f = sb("best_f", [P, 2 * TOPK])
        e_f = sb("e_f", [P, 2 * TOPK])
        gsum = sb("gsum", [P, 2])
        dots = sb("dots", [P, 2, UG])
        gl = sb("gl", [P, 2, UG])
        wts = sb("wts", [P, 2, UG])
        wdiag = diag

        block = ctx.enter_context(nc.Block())

        @block.sync
        def _(sp):
            w = T["w_stream"]
            sp.dma_start(cols[:, :], T["cols"]).then_inc(S["cols_in"], 16)
            for s in range(RING):
                sp.dma_start(ring[:, s, :], w[s]).then_inc(w_landed[s], 16)
            n = N_CHUNKS // RING
            with sp.Fori(1, n) as i:
                for s in range(RING):
                    sp.wait_ge(S["w_used"], i * RING + (s - RING + 1))
                    sp.dma_start(ring[:, s, :], w[ds(i * RING + s, 1)].rearrange("a p n -> p (a n)")).then_inc(w_landed[s], 16)
            for c in range(n * RING, N_CHUNKS):
                sp.wait_ge(S["w_used"], c - RING + 1)
                sp.dma_start(ring[:, c % RING, :], w[c]).then_inc(w_landed[c % RING], 16)
            for t in range(NT):
                sp.wait_ge(S["y_added"], t + 1)
                sp.dma_start(out[t * P:(t + 1) * P, :], x_tok[:, t, :]).then_inc(S["stored"], 16)
            sp.wait_ge(S["stored"], 16 * NT)

        @block.gpsimd
        def _(gp):
            gp.memset(ones[:, :], 1.0).then_inc(S["ones_ready"], 1)
            gp.memset(eps[:, :], EPS).then_inc(S["ones_ready"], 1)
            gp.memset(mod[:, :, :].rearrange("p a b -> p (a b)"), 0.0).then_inc(S["acc_zero"], 1)
            gp.dma_start(memT, T["memT"]).then_inc(S["mem_in"], 16)
            gp.dma_start(inv_cnt, T["inv_cnt"].to_broadcast([P, 4 * SEQ]).rearrange("p (a b) -> p a b", a=4)).then_inc(S["sgu_in"], 16)
            gp.dma_start(region(Z0 + 2048, 1024), T["sgu_rows"].to_broadcast([P, 1024])).then_inc(S["sgu_in"], 16)
            gp.dma_start(w_pool, T["w_pool"]).then_inc(S["sgu_in"], 16)
            gp.dma_start(w_spT, T["w_spT"]).then_inc(S["sgu_in"], 16)
            gp.dma_start(rows[:, :], T["rows"].to_broadcast([P, N_ROWS])).then_inc(S["rows_in"], 16)
            gp.dma_start(pos_i[:, :], T["positions"]).then_inc(S["pos_in"], 16)
            gp.wait_ge(S["acc_zero"], 1)
            gp.dma_start(mod[0:1, :, :].rearrange("p a b -> p (a b)"), T["b_ada"]).then_inc(S["ada_b_in"], 16)
            for p in range(48):
                if p >= 2:
                    gp.wait_ge(S["ada_used"], p - 1)
                k, s = p // 6, p % 6
                gp.dma_start(ada_ring[:, p % 2, :], T["w_ada"][k * P:(k + 1) * P, s * D:(s + 1) * D]).then_inc(ada_landed[p % 2], 16)
            gp.wait_ge(S["ada_used"], 48)
            gp.dma_start(sub_keys, T["sub_keys"]).then_inc(S["sub_in"], 16)
            gp.wait_ge(S["lin_evacuated"], LIN_MOD_COLS)
            gp.dma_start(sel, T["sel"]).then_inc(S["sel_in"], 16)
            gp.wait_ge(S["f_cum_ready"], 1)
            gp.dma_start(mod[:, 0, :], T["norm2_g"].to_broadcast([P, D])).then_inc(S["gn2_in"], 16)

            def gather(rows_buf, table, slot, t, j, landed):
                gp.indirect_dma_start(rows_buf[:, slot, :], None, table,
                                      bass.IndirectOffsetOnAxis(ap=idx[:, t, j:j + 1], axis=0)).then_inc(landed[slot], 16)
            n_groups = NT * ROWS_PER_TILE // UG
            per_tile = ROWS_PER_TILE // UG
            for g in range(n_groups + 1):
                if g < n_groups:
                    t, j0 = g // per_tile, g % per_tile * UG
                    if g % PER_HEAD == 0:
                        gp.wait_ge(S["top_arg"], g // PER_HEAD + 1)
                        if g == 0:
                            gp.wait_ge(S["x2_ready"], 2 * NT)
                    for s in range(UG):
                        if g >= 2:
                            gp.wait_ge(S["u_used"], UG * (g - 2) + s + 1)
                        gather(u_rows, T["peer_u"], g % 2 * UG + s, t, j0 + s, u_landed)
                if g >= 1:
                    q = g - 1
                    t, j0 = q // per_tile, q % per_tile * UG
                    for s in range(UG):
                        if q >= 2:
                            gp.wait_ge(S["v_used"], UG * (q - 2) + s + 1)
                        gather(v_rows, T["peer_v"], q % 2 * UG + s, t, j0 + s, v_landed)

        @block.tensor
        def _(pe):
            st = Steps(pe, S["pe_own"])
            chunk = [0]
            release = [0]
            lin = [0]
            loop = [None]

            mm = pe.matmul

            def mmw(o, lhsT, rhs, **kw):
                ins = pe.matmul(o, lhsT, rhs, **kw)
                if release[0]:
                    ins.then_inc(S["w_used"], release[0])
                    release[0] = 0
                return ins

            def take():
                c = chunk[0]
                chunk[0] += 1
                v = 16 * (c // RING + 1)
                if loop[0] is not None:
                    v = loop[0][0] * (16 * (loop[0][1] // RING)) + v
                pe.wait_ge(w_landed[c % RING], v)
                return ring[:, c % RING, :]

            def bank():
                n = lin[0] - 3
                if loop[0] is not None:
                    pe.wait_ge(S["lin_evacuated"], loop[0][0] * loop[0][2] + n)
                elif n > 0:
                    pe.wait_ge(S["lin_evacuated"], n)
                lin[0] += 1
                return psum[(lin[0] - 1) % 4]

            def results(ins, n=1):
                ins.then_inc(S["lin_ready"], n)

            def loops(n, chunks, outs, body):
                assert chunks % RING == 0 and outs % 4 == 0 and lin[0] >= 4 and release[0] == 1
                c0, l0 = chunk[0], lin[0]
                with pe.Fori(0, n) as i:
                    loop[0] = (i, chunks, outs)
                    body()
                    loop[0] = None
                assert chunk[0] == c0 + chunks and lin[0] == l0 + outs and release[0] == 1
                chunk[0], lin[0] = c0 + n * chunks, l0 + n * outs

            def linear_fm(src, n_chunks, kb=KB, width=SEQ, first_wait=None):
                for c in range(n_chunks):
                    w = take()
                    for m in range(KB // kb):
                        b = bank()
                        for k in range(kb):
                            if first_wait is not None and c == 0 and m == 0:
                                first_wait(k)
                            last = mmw(b[:, 0:width], w[:, (m * kb + k) * P:(m * kb + k + 1) * P], src[:, k, 0:width],
                                      start=k == 0, stop=k == kb - 1)
                        results(last)
                    release[0] += 1

            def linear_tok(src, n_chunks, width, tiles=NT, kb=KB, first_wait=None):
                banks = [bank() for _ in range(tiles)]
                for c in range(n_chunks):
                    w = take()
                    for kk in range(kb // n_chunks):
                        k = c * (kb // n_chunks) + kk
                        if first_wait is not None:
                            first_wait(k)
                        for t in range(tiles):
                            last = mmw(banks[t][:, 0:width], src[:, k, t * P:(t + 1) * P], w[:, kk * width:(kk + 1) * width],
                                      start=k == 0, stop=k == kb - 1)
                    release[0] += 1
                results(last, tiles)

            norms = [0]
            sq_seen = [0]

            def norm(nb, tiles=NT, first=0):
                for k in range(nb):
                    sq_seen[0] += 1
                    pe.wait_ge(S["sq_ready"], sq_seen[0])
                    for t in range(tiles):
                        last = mm(psum[6][:, t:t + 1], sqT[:, first + k, t * P:(t + 1) * P], ones[:, 0:1],
                                  start=k == 0 and t == 0, stop=k == nb - 1, skip_group_check=True)
                last.then_inc(S["sumsq_ready"], 1)
                norms[0] += 1
                pe.wait_ge(S["diag_ready"], norms[0])
                mm(psum[7][:, 0:tiles * P], ones[:, :], diag[:, 0:tiles, :], start=True, stop=True).then_inc(S["rbc_ready"], 1)

            h_seen = [0]

            def h_block(k):
                pe.wait_ge(S["h_ready"], h_seen[0] + k + 1)

            def attend(kind, q_of, k_of, v_of):
                units, dv = plan[kind]["units"], plan[kind]["dv"]
                n = len(units)
                pe.wait_ge(S["lin_evacuated"], lin[0])
                tile_end = {}
                for i in range(n + 5):
                    if i < n:
                        x = units[i]
                        u = x["u"]
                        if u >= 2:
                            pe.wait_ge(S["p_ready"], u - 1)
                        b0, nk = x["blocks"][0], len(x["blocks"]) * P
                        mm(psum[4 + u % 2][:, 0:nk], q_of(x), k_of(x, b0 * P, nk), start=True, stop=True).then_inc(S["s_ready"], 1)
                    if 1 <= i <= n:
                        x = units[i - 1]
                        u = x["u"]
                        pe.wait_ge(S["p_ready"], u + 1)
                        if u >= 2:
                            pe.wait_ge(S["pt_copied"], u - 1)
                        for j in range(len(x["blocks"])):
                            last = pe.transpose(psum[6 + u % 2][:, j * P:(j + 1) * P], probs[:, u % 2, j * P:(j + 1) * P], ident)
                        last.then_inc(S["pt_ready"], 1)
                    if 2 <= i <= n + 1:
                        x = units[i - 2]
                        u, g = x["u"], x["g"]
                        pe.wait_ge(S["pt_copied"], u + 1)
                        if x["h"] == 0 and g >= 2:
                            pe.wait_ge(S["o_normed"], g - 1)
                        for j, kb_ in enumerate(x["blocks"]):
                            last = mm(psum[g % 2][:, x["h"] * dv:(x["h"] + 1) * dv], probsT[:, u % 2, j * P:(j + 1) * P],
                                      v_of(x, kb_), start=j == 0, stop=j == len(x["blocks"]) - 1)
                        last.then_inc(S["av_done"], 1)
                        if x["last"]:
                            tile_end[i + 2] = g
                    if i in tile_end:
                        g = tile_end[i]
                        pe.wait_ge(S["o_normed"], g + 1)
                        if g >= 1:
                            pe.wait_ge(S["ot_copied"], g)
                        for j in range(4):
                            last = pe.transpose(psum[2][:, j * P:(j + 1) * P], o_tok[:, g % 2, j * P:(j + 1) * P], ident)
                        last.then_inc(S["ot_ready"], 1)
                assert len(tile_end) == NT
                pe.wait_ge(S["ot_copied"], units[-1]["g"] + 1)

            pe.wait_ge(S["consts_in"], 16)
            pe.wait_ge(S["ones_ready"], 2)
            norm(KB)
            norm(KB, tiles=2)
            linear_tok(hT, 1, P, first_wait=h_block)
            linear_fm(hT, 5)
            pe.wait_ge(S["mem_ready"], KB)
            linear_fm(memT, 4, width=N_MEM)
            linear_tok(memT, 4, 512, tiles=2)
            linear_tok(hT, 4, 512)
            linear_fm(hT, 8)
            h_seen[0] += KB
            attend("band",
                   lambda x: q1T[x["h"] // 4 * 64:x["h"] // 4 * 64 + 64, x["h"] % 4, x["t"] * P:(x["t"] + 1) * P],
                   lambda x, k0, nk: k1T[x["h"] // 4 * 64:x["h"] // 4 * 64 + 64, k0:k0 + nk],
                   lambda x, b: v1[:, b, x["h"] // 4 * 64:x["h"] // 4 * 64 + 64])
            pe.wait_ge(S["vs_ready"], NT)
            pe.wait_ge(S["wsp_ready"], 1)
            for g in range(4):
                b = bank()
                for t in range(NT):
                    last = mm(b[:, t * P:(t + 1) * P], vS[:, t, g * P:(g + 1) * P], w_spT[:, g, :], start=True, stop=True)
                results(last)
            pe.wait_ge(S["pooled_ready"], 4)
            for g in range(4):
                b = bank()
                results(mm(b[:, :], w_pool[:, g, :], cT[:, g, POOL_PAD:], start=True, stop=True))
            ybT = uT
            for n, y in enumerate((yaT, ybT, ycT)):
                loops(2, 4, 4, lambda: linear_fm(hT, 4))
                if n == 1:
                    pe.wait_ge(S["yb_ready"], 4)
                if n == 2:
                    pe.wait_ge(S["lin_evacuated"], lin[0])
                linear_fm(y, 4, kb=4)
            pe.wait_ge(S["merged_ready"], 3 * KB)
            loops(2, 4, 4, lambda: linear_fm(merged, 4))
            norm(KB)
            norm(KB)
            linear_fm(hT, 4, first_wait=h_block)
            h_seen[0] += KB
            attend("mem",
                   lambda x: qmT[:, x["h"], x["t"] * P:(x["t"] + 1) * P],
                   lambda x, k0, nk: kmT[:, x["h"], 0:nk],
                   lambda x, b: vm[:, b, x["h"] * P:(x["h"] + 1) * P])
            linear_fm(ymT, 4, kb=4)
            norm(KB)
            norm(KB)
            for k in range(KB):
                h_block(k)
            h_seen[0] += KB
            loops(8, 4, 4, lambda: linear_fm(hT, 4))
            pe.wait_ge(S["hid_ready"], FF_BLOCKS)

            def down():
                for m in range(4):
                    b = bank()
                    for q in range(4):
                        w = take()
                        for k in range(KB):
                            last = mmw(b[:, :], w[:, k * P:(k + 1) * P], hid[:, q * KB + k, :],
                                      start=q == 0 and k == 0, stop=q == 3 and k == KB - 1)
                        release[0] += 1
                    results(last)
            loops(2, 16, 4, down)
            norm(KB)
            pe.wait_ge(S["ada_used"], 48)
            b = bank()
            for j in range(2 * KB):
                last = mm(b[:, j:j + 1], mod[:, 0:2, :].rearrange("p a b -> p (a b)")[:, j * P:(j + 1) * P], ones[:, 0:1],
                          start=True, stop=True)
            results(last)
            for s in range(2, 6):
                for half in range(2):
                    b = bank()
                    results(mm(b[:, :], ones[:, :], mod[:, s, half * 512:(half + 1) * 512], start=True, stop=True))
            norm(KB)
            linear_fm(hT, 5, first_wait=h_block)
            linear_tok(hT, 1, 40)
            for _ in range(3):
                linear_tok(hT, 4, 512)
            h_seen[0] += KB
            norm(3)
            norm(2, first=3)
            pe.wait_ge(S["cqn_ready"], 5)
            ws = []
            for half in range(2):
                banks = [bank() for _ in range(NT)]
                for k in range(3):
                    if half == 0:
                        ws.append(take())
                    for t in range(NT):
                        last = mmw(banks[t][:, 0:384], cqT[:, k, t * P:(t + 1) * P], ws[k][:, half * 384:(half + 1) * 384],
                                  start=k == 0, stop=k == 2)
                results(last, NT)
            release[0] += 3
            ws = []
            for half in range(2):
                banks = [bank() for _ in range(NT)]
                for k in range(2):
                    if half == 0:
                        ws.append(take())
                    for t in range(NT):
                        last = mmw(banks[t][:, :], cqT[:, 3 + k, t * P:(t + 1) * P], ws[k][:, half * 512:(half + 1) * 512],
                                  start=k == 0, stop=k == 1)
                results(last, NT)
            release[0] += 2
            pe.wait_ge(S["fl_ready"], 1)
            b = bank()
            for t in range(NT):
                last = pe.transpose(b[0:HEADS, t * P:(t + 1) * P], fl_a[:, t * HEADS:(t + 1) * HEADS], ident)
            results(last)
            pe.wait_ge(S["f_cum_ready"], 1)
            b = bank()
            for t in range(NT):
                last = pe.transpose(b[:, t * HEADS:(t + 1) * HEADS], f_cum[:, t * P:(t + 1) * P], ident[0:HEADS, 0:HEADS])
            results(last)
            pe.wait_ge(S["sel_in"], 16)
            for h in range(HEADS):
                b = bank()
                results(mm(b[:, :], sel[:, h * P:(h + 1) * P], f_cum, start=True, stop=True))
            for n, src in enumerate((fq_tok, fk_tok)):
                pe.wait_ge(S["tok_ready"], n + 1)
                for j in range(4):
                    b = bank()
                    for t in range(NT):
                        last = pe.transpose(b[:, t * P:(t + 1) * P], src[:, t, j * P:(j + 1) * P], ident)
                    results(last)
            for n, src in enumerate((k_tok, q_tok)):
                pe.wait_ge(S["tok_ready"], n + 3)
                if n == 1:
                    pe.wait_ge(S["lin_evacuated"], lin[0])
                for h in range(HEADS):
                    b = bank()
                    for t in range(NT):
                        last = pe.transpose(b[0:QK, t * P:(t + 1) * P], src[:, t, h, :], ident)
                    results(last)
            attend("mla",
                   lambda x: qT[0:QK, x["h"], x["t"] * P:(x["t"] + 1) * P],
                   lambda x, k0, nk: kT[0:QK, x["h"], k0:k0 + nk],
                   lambda x, b: v_mla[:, b, x["h"] * 64:(x["h"] + 1) * 64])
            attend("fox",
                   lambda x: fqT[x["h"] % 2 * 64:x["h"] % 2 * 64 + 64, x["h"] // 2, x["t"] * P:(x["t"] + 1) * P],
                   lambda x, k0, nk: fkT[x["h"] % 2 * 64:x["h"] % 2 * 64 + 64, x["h"] // 2, k0:k0 + nk],
                   lambda x, b: v_fox[:, b, x["h"] * 64:(x["h"] + 1) * 64])
            for t in range(NT):
                for half in range(2):
                    b = bank()
                    for j in range(4):
                        last = pe.transpose(b[:, j * P:(j + 1) * P], xT[:, half * 4 + j, t * P:(t + 1) * P], ident)
                    results(last)
            linear_tok(oT, 4, 512)
            linear_tok(oT, 4, 512)
            for t in range(NT):
                pe.wait_ge(S["h2_ready"], t + 1)
                for half in range(2):
                    b = bank()
                    for j in range(4):
                        last = pe.transpose(b[:, j * P:(j + 1) * P], h2_tok[:, t, (half * 4 + j) * P:(half * 4 + j + 1) * P], ident)
                    results(last)
            pe.wait_ge(S["lin_evacuated"], lin[0])
            pe.wait_ge(S["sub_in"], 16)

            def key_scores(n):
                t, h = n // HEADS, n % HEADS
                if n >= 2:
                    pe.wait_ge(S["sc_copied"], n - 1)
                for p in range(2):
                    last = mm(psum[4 + n % 2][:, p * P:(p + 1) * P], qpT[:, 2 * h + p, t * P:(t + 1) * P],
                              sub_keys[:, 2 * h + p, :], start=True, stop=True)
                last.then_inc(S["sc_ready"], 1)

            def group(t, reg, q, first=False, last_group=False):
                y = [psum[(6, 0)[t % 2] + half] for half in range(2)]
                for s in range(UG):
                    n = t * per_tile + q
                    v = 16 * (n // 2 + 1)
                    dg = n * UG + s + 1
                    if reg is not None:
                        v = reg * 16 + v
                        dg = reg * (2 * UG) + dg
                    pe.wait_ge(v_landed[q % 2 * UG + s], v)
                    pe.wait_ge(S["dg_ready"], dg)
                    for half in range(2):
                        ins = mm(y[half][:, :], wdiag[:, s, :], v_rows[:, q % 2 * UG + s, half * 512:(half + 1) * 512],
                                 start=first and s == 0, stop=last_group and s == UG - 1)
                    ins.then_inc(S["v_used"], 1)
            per_tile = ROWS_PER_TILE // UG

            for h in range(HEADS):
                linear_fm(h2T, 2)
                pe.wait_ge(S["lin_evacuated"], lin[0])
                key_scores(h)
                if h >= HEADS - EARLY:
                    g = h - (HEADS - EARLY)
                    group(0, None, g, first=g == 0)
            for t in range(NT):
                if t + 1 < NT:
                    for h in range(HEADS):
                        key_scores(HEADS * (t + 1) + h)
                if t >= 2:
                    pe.wait_ge(S["y_added"], t - 1)
                head = EARLY if t == 0 else 2
                if t:
                    group(t, None, 0, first=True)
                    group(t, None, 1)
                with pe.Fori(0, (per_tile - head) // 2 - 1) as i:
                    group(t, i, head)
                    group(t, i, head + 1)
                group(t, None, per_tile - 2)
                group(t, None, per_tile - 1, last_group=True)

        @block.scalar
        def _(ac):
            st = Steps(ac, S["act_own"])
            lin = [0]
            loop = [None]

            def ready(n=1):
                lin[0] += n
                v = lin[0]
                if loop[0] is not None:
                    v = loop[0][0] * loop[0][1] + v
                ac.wait_ge(S["lin_ready"], v)
                return psum[(lin[0] - 1) % 4]

            def evac(dst, func=ACT.Copy, width=512, rows_=P, src=None, **kw):
                b = ready()
                s = b[0:rows_, 0:width] if src is None else src(b)
                ac.activation(dst, s, func, **kw).then_inc(S["lin_evacuated"], 1)

            def squares(src_of, nb, width=SEQ, wait=None):
                for k in range(nb):
                    if wait is not None:
                        wait(k)
                    ac.activation(sqT[:, k, 0:width], src_of(k), ACT.Square).then_inc(S["sq_ready"], 1)

            norms = [0]

            def norm_std(width, tiles=NT):
                norms[0] += 1
                ac.wait_ge(S["sumsq_ready"], norms[0])
                ac.activation(std[:, 0:tiles], psum[6][:, 0:tiles], ACT.Sqrt, scale=1.0 / width, bias=eps[:, 0:1])\
                  .then_inc(S["std_ready"], 1)

            ac.dma_start(xT, T["xT"]).then_inc(S["x_in"], 16)
            ac.dma_start(cst[:, :], T["cst"]).then_inc(S["consts_in"], 16)
            ac.wait_ge(S["x_in"], 16)
            squares(lambda k: xT[:, k, :], KB)
            ac.wait_ge(S["ones_ready"], 2)
            norm_std(D)
            ac.wait_ge(S["mem_in"], 16)
            squares(lambda k: memT[:, k, :], KB, width=N_MEM)
            norm_std(D, tiles=2)
            ac.wait_ge(S["cols_in"], 16)
            ac.activation(silu_c[:, :], cols[:, COLS["c"]], ACT.Sigmoid).then_inc(S["sig_c"], 1)
            for t in range(NT):
                evac(v1[:, t, :], width=P)
            for j in range(4):
                evac(q1T[:, j, :], scale=0.125)
            evac(k1T)
            for j in range(4):
                evac(kmT[:, j, :], width=N_MEM)
            for j in range(2):
                evac(vm[:, j, :])
            for t in range(NT):
                evac(vS[:, t, :], ACT.Gelu_apprx_tanh)
            for j in range(4):
                evac(uT[:, j, :], ACT.Gelu_apprx_tanh)
            for j in range(4):
                evac(cT[:, j, POOL_PAD:])
            ac.wait_ge(S["v_sq_ready"], NT)
            ac.activation(std[:, :], rstd[:, :], ACT.Sqrt, scale=1.0 / 512, bias=eps[:, 0:1]).then_inc(S["vstd_ready"], 1)

            def attend(kind, scale, dst):
                units, heads = plan[kind]["units"], plan[kind]["heads"]
                n = len(units)
                tile_end = {}
                for i in range(n + 5):
                    if i < n:
                        x = units[i]
                        u, pr = x["u"], x["g"] % 2
                        nk = len(x["blocks"]) * P
                        ac.wait_ge(S["neg_ready"], u + 1)
                        if u >= 2:
                            ac.wait_ge(S["pt_ready"], u - 1)
                        ac.activation(probs[:, u % 2, 0:nk], psum[4 + u % 2][:, 0:nk], ACT.Exp, scale=scale,
                                      bias=neg_m[:, pr, x["h"]:x["h"] + 1],
                                      accum_out=row_sum[:, pr, x["h"]:x["h"] + 1]).then_inc(S["p_ready"], 1)
                        if kind == "band" and x["last"]:
                            ac.wait_ge(S["sink_arg"], x["t"] + 1)
                            ac.activation(sink_e[:, pr, :], sink_e[:, pr, :], ACT.Exp).then_inc(S["sink_exp"], 1)
                    if 1 <= i <= n:
                        x = units[i - 1]
                        u = x["u"]
                        nk = len(x["blocks"]) * P
                        ac.wait_ge(S["pt_ready"], u + 1)
                        if u >= 2:
                            ac.wait_ge(S["av_done"], u - 1)
                        ac.activation(probsT[:, u % 2, 0:nk], psum[6 + u % 2][:, 0:nk], ACT.Copy).then_inc(S["pt_copied"], 1)
                        if x["last"]:
                            tile_end[i + 3] = (x["g"], x["t"])
                    if i in tile_end:
                        g, t = tile_end[i]
                        ac.wait_ge(S["ot_ready"], g + 1)
                        ac.activation(dst[:, 0:4, t * P:(t + 1) * P],
                                      psum[2][:, :].rearrange("p (a b) -> p a b", a=4), ACT.Copy).then_inc(S["ot_copied"], 1)
                assert len(tile_end) == NT

            attend("band", 1.0, yaT)
            for g in range(4):
                evac(sqT[:, 4 + g, :])
            for g in range(4):
                evac(ycT[:, g, :], scale=cols[:, COLS["pool_scale"]][:, g:g + 1])
            for n in range(3):
                if n == 0:
                    ac.wait_ge(S["yb_ready"], 4)
                    ac.wait_ge(S["mem_ready"], KB)
                else:
                    ac.wait_ge(S["merged_ready"], KB * n)
                with ac.Fori(0, 2) as i:
                    loop[0] = (i, 4)
                    for s in range(4):
                        evac(gates[:, ds(i * 4 + s, 1), :].rearrange("p a b -> p (a b)"), ACT.Sigmoid)
                    loop[0] = None
                lin[0] += 4
                for k in range(KB):
                    evac(sqT[:, k, :])

            def z_evac(k):
                b = ready()
                ac.activation(sqT[:, k, :], b[:, :], ACT.Square).then_inc(S["sq_ready"], 1)
                ac.activation(zT[:, k, :], b[:, :], ACT.Copy).then_inc(S["lin_evacuated"], 1)

            def residual_norms(k):
                squares(lambda b: xT[:, b, :], KB, wait=lambda b: ac.wait_ge(S["x_ready"], KB * k + b + 1))
            ac.wait_ge(S["merged_ready"], 3 * KB)
            for k in range(KB):
                z_evac(k)
            norm_std(D)
            residual_norms(0)
            norm_std(D)
            for j in range(4):
                evac(qmT[:, j, :])
            attend("mem", 1.0 / math.sqrt(128), ymT)
            for k in range(KB):
                z_evac(k)
            norm_std(D)
            residual_norms(1)
            norm_std(D)
            with ac.Fori(0, 8) as i:
                loop[0] = (i, 4)
                for s in range(4):
                    evac(hid[:, ds(i * 4 + s, 1), :].rearrange("p a b -> p (a b)"), ACT.Relu)
                loop[0] = None
            lin[0] += 28
            for k in range(KB):
                z_evac(k)
            norm_std(D)
            evac(mod_cols[:, :], width=2 * KB)
            for s in range(2, 6):
                for half in range(2):
                    evac(mod[:, s, half * 512:(half + 1) * 512])
            residual_norms(2)
            norm_std(D)
            for k in range(5):
                b = ready()
                ac.activation(sqT[:, k, :], b[:, :], ACT.Square).then_inc(S["sq_ready"], 1)
                ac.activation(cqT[:, k, :], b[:, :], ACT.Copy).then_inc(S["lin_evacuated"], 1)
            for t in range(NT):
                evac(misc_tok[:, t, :], width=40)
            for dst in (fq_tok, fk_tok, v_fox):
                for t in range(NT):
                    evac(dst[:, t, :])
            norm_std(384)
            norm_std(256)
            for half in range(2):
                for t in range(NT):
                    evac(q_tok[:, t, :, :].rearrange("p h d -> p (h d)")[:, half * 384:(half + 1) * 384], width=384)
            for t in range(NT):
                evac(k_tok[:, t, :, 0:64], src=lambda b: b[:, :].rearrange("p (h d) -> p h d", h=HEADS))
            for t in range(NT):
                evac(v_mla[:, t, :])
            ac.wait_ge(S["fl_arg"], 1)
            ac.activation(fl_b, fl_b, ACT.Exp, scale=-1.0).then_inc(S["fl_exp"], 1)
            ac.wait_ge(S["fl_exp"], 1)
            ac.activation(fl_b, fl_b, ACT.Ln, bias=ones[:, 0:1]).then_inc(S["fl_exp"], 1)
            evac(f_log, rows_=HEADS)
            evac(sm(548, 32), width=32)
            for h in range(HEADS):
                evac(f_row[:, h, :])
            ac.wait_ge(S["trig_arg"], 1)
            ac.activation(sin_t, sin_t, ACT.Sin).then_inc(S["trig_ready"], 1)
            ac.activation(cos_t, cos_t, ACT.Sin).then_inc(S["trig_ready"], 1)
            for n, (src, width) in enumerate(((fq_tok, 64), (fk_tok, 64), (k_tok, QK), (q_tok, QK))):
                if n == 2:
                    ac.wait_ge(S["tok_sq"], 1)
                if n >= 1:
                    ac.wait_ge(S["tok_ss"], n)
                flat = src.rearrange("p t n -> p (t n)") if n < 2 else src.rearrange("p t h d -> p (t h d)")
                ac.activation(sq_tok.rearrange("p t n -> p (t n)")[:, 0:NT * HEADS * width], flat, ACT.Square)\
                  .then_inc(S["tok_std"], 1)
                ac.wait_ge(S["tok_ss"], n + 1)
                ac.activation(r_tok, ss_tok, ACT.Sqrt, scale=1.0 / width, bias=eps[:, 0:1]).then_inc(S["tok_std"], 1)
                if n < 2:
                    for j in range(4):
                        evac((fqT, fkT)[n][:, j, :])
                else:
                    for h in range(HEADS):
                        evac((kT, qT)[n - 2][0:QK, h, :], rows_=QK)
            attend("mla", QK ** -0.5, oT[:, 0:4, :])
            attend("fox", 1.0, oT[:, 4:8, :])
            for t in range(NT):
                for half in range(2):
                    evac(h2_tok[:, t, half * 512:(half + 1) * 512])
            for half in range(2):
                for t in range(NT):
                    evac(x_tok[:, t, half * 512:(half + 1) * 512])
            for t in range(NT):
                ac.wait_ge(S["x2_ready"], NT + t + 1)
                ac.activation(h2_tok[:, t, :], x_tok[:, t, :], ACT.Square, accum_out=std[:, t:t + 1]).then_inc(S["h2_sq"], 1)
                ac.wait_ge(S["h2_sq"], t + 1)
                ac.activation(rstd[:, t:t + 1], std[:, t:t + 1], ACT.Sqrt, scale=1.0 / D, bias=eps[:, 0:1]).then_inc(S["h2_std"], 1)
            for t in range(NT):
                for half in range(2):
                    b = ready()
                    ac.activation(h2T[:, half * 4:half * 4 + 4, t * P:(t + 1) * P],
                                  b[:, :].rearrange("p (a b) -> p a b", a=4), ACT.Copy).then_inc(S["lin_evacuated"], 1)

            def key_scores(n):
                if n % HEADS == 0 and n >= 2 * HEADS:
                    ac.wait_ge(S["top_arg"], n - HEADS)
                h = n % HEADS
                ac.wait_ge(S["sc_ready"], n + 1)
                ac.activation(scores[n // HEADS % 2][:, 2 * h * P:2 * (h + 1) * P], psum[4 + n % 2][:, 0:2 * P], ACT.Copy)\
                  .then_inc(S["sc_copied"], 1)

            def gate_exp(n):
                ac.wait_ge(S["top_arg"], n + 1)
                t, h = n // HEADS, n % HEADS
                g = gate_w[:, t % 2, h * TOPK:(h + 1) * TOPK]
                ac.activation(g, g, ACT.Exp, accum_out=gsum[:, n % 2:n % 2 + 1]).then_inc(S["top_exp"], 1)

            def group(n):
                ac.wait_ge(S["u_used"], UG * (n + 1))
                if n >= 2:
                    ac.wait_ge(S["w_ready"], n - 1)
                ac.activation(gl[:, n % 2, :], dots[:, n % 2, :], ACT.Gelu_apprx_tanh).then_inc(S["gl_ready"], 1)
                if n % PER_HEAD == 2 and n // PER_HEAD + 2 < NT * HEADS:
                    gate_exp(n // PER_HEAD + 2)
                ac.wait_ge(S["w_ready"], n + 1)
                for s in range(UG):
                    if n >= 1:
                        ac.wait_ge(S["v_used"], UG * (n - 1) + s + 1)
                    ac.activation(wdiag[:, s, :], ident, ACT.Copy, scale=wts[:, n % 2, s:s + 1]).then_inc(S["dg_ready"], 1)
            for h in range(HEADS):
                for p in range(2):
                    evac(qpT[:, 2 * h + p, :])
                key_scores(h)
                if h < 2:
                    gate_exp(h)
                if h >= HEADS - EARLY:
                    group(h - (HEADS - EARLY))
            per_tile = ROWS_PER_TILE // UG
            for t in range(NT):
                if t + 1 < NT:
                    for h in range(HEADS):
                        key_scores(HEADS * (t + 1) + h)
                for q in range(EARLY if t == 0 else 0, per_tile):
                    group(t * per_tile + q)

        @block.vector
        def _(ve):
            st = Steps(ve, S["dve_own"])
            norms = [0]

            def spread(n_tiles=NT):
                norms[0] += 1
                ve.wait_ge(S["std_ready"], norms[0])
                st(ve.reciprocal(rstd[:, 0:n_tiles], std[:, 0:n_tiles]))
                st(ve.tensor_tensor(diag[:, 0:n_tiles, :], ident.unsqueeze(1).to_broadcast([P, n_tiles, P]),
                                    rstd[:, 0:n_tiles].unsqueeze(2).to_broadcast([P, n_tiles, P]), ALU.mult), S["diag_ready"])
                ve.wait_ge(S["rbc_ready"], norms[0])

            def scale_blocks(dst, src, gain, nb, sem_, width=SEQ):
                for k in range(nb):
                    st(ve.scalar_tensor_tensor(dst[:, k, :], src[:, k, :], gain[:, k:k + 1], psum[7][:, 0:width],
                                               ALU.mult, ALU.mult), sem_)

            def residual(gain, evacuated):
                spread()
                ve.wait_ge(S["lin_evacuated"], evacuated)
                for k in range(KB):
                    st(ve.scalar_tensor_tensor(zT[:, k, :], zT[:, k, :], gain[:, k:k + 1], psum[7][:, :], ALU.mult, ALU.mult))
                    st(ve.tensor_tensor(xT[:, k, :], xT[:, k, :], zT[:, k, :], ALU.add), S["x_ready"])

            ve.wait_ge(S["cols_in"], 16)
            ve.wait_ge(S["consts_in"], 16)
            ve.wait_ge(S["x_in"], 16)
            spread()
            scale_blocks(hT, xT, cols[:, COLS["g0"]], KB, S["h_ready"])
            spread(2)
            scale_blocks(memT, memT, cols[:, COLS["g_mem"]], KB, S["mem_ready"], width=N_MEM)
            ve.wait_ge(S["sig_c"], 1)
            st(ve.tensor_tensor(silu_c[:, :], silu_c[:, :], cols[:, COLS["c"]], ALU.mult), S["silu_ready"])
            st(ve.memset(cT[:, :, 0:POOL_PAD], 0.0))
            st(ve.memset(pool_a[:, 0:POOL_PAD], 0.0))
            st(ve.memset(pool_b[:, 0:POOL_PAD], 0.0))
            ve.wait_ge(S["sgu_in"], 64)
            st(ve.memset(w_spT[64:P, :, 0:64], 0.0), S["wsp_ready"])
            for t in range(NT):
                ve.wait_ge(S["lin_evacuated"], 15 + t + 1)
                st(ve.tensor_tensor(sqT[:, 4 + t, :], vS[:, t, :], vS[:, t, :], ALU.mult))
                st(ve.reduce_sum(rstd[:, t:t + 1], sqT[:, 4 + t, :], axis=AX_X), S["v_sq_ready"])
            ve.wait_ge(S["vstd_ready"], 1)
            st(ve.reciprocal(rstd[:, :], std[:, :]))
            for t in range(NT):
                st(ve.scalar_tensor_tensor(vS[:, t, :], vS[:, t, :], rstd[:, t:t + 1], g_sgu_row, ALU.mult, ALU.mult), S["vs_ready"])
            for g in range(4):
                ve.wait_ge(S["lin_evacuated"], 23 + g + 1)
                src = cT[:, g, :]
                for lvl in range(g + 1):
                    dst = (pool_a, pool_b)[lvl % 2]
                    sh = 1 << lvl
                    st(ve.tensor_tensor(dst[:, POOL_PAD:], src[:, POOL_PAD:], src[:, POOL_PAD - sh:POOL_PAD - sh + SEQ], ALU.add))
                    src = dst
                st(ve.tensor_tensor(src[:, POOL_PAD:], src[:, POOL_PAD:], inv_cnt[:, g, :], ALU.mult))
                st(ve.tensor_tensor(cT[:, g, POOL_PAD:], src[:, POOL_PAD:], cT[:, g, POOL_PAD:], ALU.subtract), S["pooled_ready"])

            def attend(kind):
                units, heads = plan[kind]["units"], plan[kind]["heads"]
                dv = 512 // heads
                n = len(units)
                tile_end = {}
                for i in range(n + 4):
                    if i < n:
                        x = units[i]
                        u, h, t, pr = x["u"], x["h"], x["t"], x["g"] % 2
                        nk = len(x["blocks"]) * P
                        s = psum[4 + u % 2]
                        ve.wait_ge(S["s_ready"], u + 1)
                        if kind == "band":
                            st(ve.tensor_tensor(s[:, 0:nk], s[:, 0:nk], cst[:, CST["mask_band"]][:, 256 - nk:256], ALU.add))
                        elif kind == "mla":
                            st(ve.tensor_tensor(s[:, nk - P:nk], s[:, nk - P:nk], cst[:, CST["mask_diag"]], ALU.add))
                        elif kind == "fox":
                            st(ve.scalar_tensor_tensor(s[:, 0:nk], s[:, 0:nk], fq_col[:, t, h:h + 1], f_row[:, h, 0:nk],
                                                       ALU.add, ALU.subtract))
                            st(ve.tensor_tensor(s[:, nk - P:nk], s[:, nk - P:nk], cst[:, CST["mask_diag"]], ALU.add))
                        st(ve.reduce_max(mx[:, pr, h:h + 1], s[:, 0:nk], axis=AX_X))
                        if kind == "band":
                            st(ve.tensor_scalar(neg_m[:, pr, h:h + 1], mx[:, pr, h:h + 1], rows[:, ROWS["sinks"]][:, h:h + 1],
                                                -1.0, ALU.max, ALU.mult), S["neg_ready"])
                        else:
                            sc = {"mem": 1.0 / math.sqrt(128), "mla": QK ** -0.5, "fox": 1.0}[kind]
                            st(ve.tensor_scalar(neg_m[:, pr, h:h + 1], mx[:, pr, h:h + 1], -sc, None, ALU.mult), S["neg_ready"])
                        if x["last"]:
                            tile_end[i + 3] = x
                            if kind == "band":
                                st(ve.tensor_tensor(sink_e[:, pr, :], neg_m[:, pr, :], rows[:, ROWS["sinks"]], ALU.add), S["sink_arg"])
                    if i in tile_end:
                        x = tile_end[i]
                        g, pr = x["g"], x["g"] % 2
                        ve.wait_ge(S["av_done"], x["u"] + 1)
                        if kind == "band":
                            ve.wait_ge(S["sink_exp"], x["t"] + 1)
                            st(ve.tensor_tensor(row_sum[:, pr, :], row_sum[:, pr, :], sink_e[:, pr, :], ALU.add))
                        st(ve.reciprocal(row_sum[:, pr, 0:heads], row_sum[:, pr, 0:heads]))
                        if g >= 2:
                            ve.wait_ge(S["ot_ready"], g - 1)
                        st(ve.tensor_tensor(o_tok[:, g % 2, :].rearrange("p (h d) -> p h d", h=heads),
                                            psum[g % 2][:, :].rearrange("p (h d) -> p h d", h=heads),
                                            row_sum[:, pr, 0:heads].unsqueeze(2).to_broadcast([P, heads, dv]), ALU.mult), S["o_normed"])
                assert len(tile_end) == NT

            ve.wait_ge(S["rows_in"], 16)
            attend("band")
            for g in range(4):
                ve.wait_ge(S["lin_evacuated"], 27 + g + 1)
                sp = sqT[:, 4 + g, :].rearrange("p (t i) -> p t i", t=NT)
                st(ve.tensor_tensor(sp, sp, b_sp_row[:, g, :].unsqueeze(1).to_broadcast([P, NT, P]), ALU.add))
                st(ve.tensor_tensor(uT[:, g, :], uT[:, g, :], sqT[:, 4 + g, :], ALU.mult), S["yb_ready"])
            base = 35
            for n in range(3):
                for k in range(KB):
                    ve.wait_ge(S["lin_evacuated"], base + 16 * n + KB + k + 1)
                    if n == 0:
                        st(ve.tensor_tensor(merged[:, k, :], gates[:, k, :], sqT[:, k, :], ALU.mult), S["merged_ready"])
                    else:
                        st(ve.tensor_tensor(sqT[:, k, :], gates[:, k, :], sqT[:, k, :], ALU.mult))
                        st(ve.tensor_tensor(merged[:, k, :], merged[:, k, :], sqT[:, k, :], ALU.add), S["merged_ready"])
            base += 48 + KB
            residual(cols[:, COLS["g1"]], base)
            spread()
            scale_blocks(hT, xT, cols[:, COLS["g2"]], KB, S["h_ready"])
            base += 4
            attend("mem")
            base += KB
            residual(cols[:, COLS["g3"]], base)
            spread()
            scale_blocks(hT, xT, cols[:, COLS["g4"]], KB, S["h_ready"])
            ve.wait_ge(S["ada_b_in"], 16)
            with ve.Fori(0, 8) as i:
                st.enter(i, ((S["dve_own"], 1), (S["hid_ready"], 4), (S["ada_used"], 6)))
                st(ve.tensor_copy(c_now[:, :], silu_c[:, ds(i, 1)]))
                for s in range(6):
                    if s >= 2:
                        ve.wait_ge(S["lin_evacuated"], i * 4 + (base + s - 1))
                        h_ = hid[:, ds(i * 4 + (s - 2), 1), :].rearrange("p a b -> p (a b)")
                        st(ve.tensor_tensor(h_, h_, h_, ALU.mult), S["hid_ready"])
                    ve.wait_ge(ada_landed[s % 2], i * 48 + 16 * (s // 2 + 1))
                    st(ve.scalar_tensor_tensor(mod[:, s, :], ada_ring[:, s % 2, :], c_now[:, 0:1], mod[:, s, :],
                                               ALU.mult, ALU.add), S["ada_used"])
            st.leave(8)
            base += 32 + KB
            residual(cols[:, COLS["g5"]], base)
            base += 9
            ve.wait_ge(S["lin_evacuated"], base - 8)
            st(ve.scalar_tensor_tensor(mod_cols[:, KB:], mod_cols[:, KB:], 1.0, cols[:, COLS["norm1_g"]], ALU.add, ALU.mult))
            spread()
            for k in range(KB):
                st(ve.scalar_tensor_tensor(hT[:, k, :], xT[:, k, :], mod_cols[:, KB + k:KB + k + 1], psum[7][:, :], ALU.mult, ALU.mult))
                st(ve.tensor_scalar(hT[:, k, :], hT[:, k, :], mod_cols[:, k:k + 1], None, ALU.add), S["h_ready"])
            ve.wait_ge(S["pos_in"], 16)
            st(ve.tensor_copy(pos_f, pos_i[:, :]))
            a3 = ang.rearrange("p (t n) -> p t n", t=NT)
            st(ve.tensor_tensor(a3, pos_f.unsqueeze(2).to_broadcast([P, NT, ROPE_HALF]),
                                cst[:, CST["inv_freq"]].unsqueeze(1).to_broadcast([P, NT, ROPE_HALF]), ALU.mult))
            st(ve.tensor_scalar(turns, ang, 1.0 / (2 * math.pi), MAGIC, ALU.mult, ALU.add))
            st(ve.tensor_scalar(turns, turns, -MAGIC, None, ALU.add))
            for part in (TWO_PI_A, TWO_PI_B, TWO_PI_C):
                st(ve.scalar_tensor_tensor(ang, turns, -part, ang, ALU.mult, ALU.add))
            lim = 3.1415925
            st(ve.tensor_scalar(sin_t, ang, lim, -lim, ALU.min, ALU.max))
            st(ve.tensor_scalar(cos_t, ang, math.pi / 2, None, ALU.add))
            st(ve.tensor_scalar(turns, cos_t, math.pi, -2 * math.pi, ALU.is_gt, ALU.mult))
            st(ve.tensor_tensor(cos_t, cos_t, turns, ALU.add))
            st(ve.tensor_scalar(cos_t, cos_t, lim, -lim, ALU.min, ALU.max), S["trig_arg"])
            st(ve.tensor_scalar(rows[:, ROWS["fox_q_g"]], rows[:, ROWS["fox_q_g"]], 0.125, None, ALU.mult))
            spread()
            ve.wait_ge(S["lin_evacuated"], base + 5)
            for k in range(3):
                st(ve.scalar_tensor_tensor(cqT[:, k, :], cqT[:, k, :], cols[:, COLS["qa_g"]][:, k:k + 1], psum[7][:, :],
                                           ALU.mult, ALU.mult), S["cqn_ready"])
            spread()
            for k in range(2):
                st(ve.scalar_tensor_tensor(cqT[:, 3 + k, :], cqT[:, 3 + k, :], cols[:, COLS["kva_g"]][:, k:k + 1], psum[7][:, :],
                                           ALU.mult, ALU.mult), S["cqn_ready"])
            base += 5 + 4 + 12
            z3 = fl_a.rearrange("p (t h) -> p t h", t=NT)
            st(ve.tensor_tensor(z3, misc_tok[:, :, 32:40], rows[:, ROWS["b_f"]].unsqueeze(1).to_broadcast([P, NT, HEADS]), ALU.add))
            st(ve.tensor_scalar(fl_b, fl_a, -1.0, None, ALU.mult))
            st(ve.tensor_tensor(fl_b, fl_b, fl_a, ALU.max), S["fl_arg"])
            ve.wait_ge(S["fl_exp"], 2)
            st(ve.scalar_tensor_tensor(fl_a, fl_a, 0.0, fl_b, ALU.min, ALU.subtract), S["fl_ready"])
            base += 16
            ve.wait_ge(S["lin_evacuated"], base + 1)
            st(ve.tensor_tensor_scan(f_cum, ones[0:HEADS, 0:1].to_broadcast([HEADS, SEQ]), f_log, 0.0, ALU.mult, ALU.add), S["f_cum_ready"])
            base += 10
            for n in range(4):
                src, gain, dd = ((fq_tok, "fox_q_g", 64), (fk_tok, "fox_k_g", 64), (k_tok, "mla_k_g", QK), (q_tok, "mla_q_g", QK))[n]
                flat = src.rearrange("p t n -> p (t n)") if n < 2 else src.rearrange("p t h d -> p (t h d)")
                v = flat.rearrange("p (a d) -> p a d", d=dd)
                ve.wait_ge(S["tok_std"], 2 * n + 1)
                st(ve.reduce_sum(ss_tok, sq_tok.rearrange("p t n -> p (t n)")[:, 0:32 * dd].rearrange("p (a d) -> p a d", d=dd), axis=AX_X),
                   S["tok_ss"])
                ve.wait_ge(S["tok_std"], 2 * n + 2)
                st(ve.reciprocal(r_tok, r_tok))
                st(ve.tensor_tensor(v, v, r_tok.unsqueeze(2).to_broadcast([P, 32, dd]), ALU.mult))
                st(ve.tensor_tensor(v, v, rows[:, ROWS[gain]].unsqueeze(1).to_broadcast([P, 32, dd]), ALU.mult),
                   S["tok_ready"] if n < 2 else None)
                if n == 1:
                    for t in range(NT):
                        st(ve.tensor_copy(k_tok[:, t, :, 64:QK], misc_tok[:, t, 0:32].unsqueeze(1).to_broadcast([P, HEADS, 32])),
                           S["tok_sq"] if t == NT - 1 else None)
                if n >= 2:
                    if n == 2:
                        ve.wait_ge(S["trig_ready"], 2)
                    tmp = sq_tok.rearrange("p t n -> p (t n)")
                    x1, x2 = src[:, :, :, 64:80], src[:, :, :, 80:96]
                    tm = [tmp[:, q * 512:(q + 1) * 512].rearrange("p (t h d) -> p t h d", t=NT, h=HEADS) for q in range(4)]
                    for q, (a, trig) in enumerate(((x1, cos_t), (x2, sin_t), (x2, cos_t), (x1, sin_t))):
                        for t in range(NT):
                            tr = trig.rearrange("p (t d) -> p t d", t=NT)[:, t, :].unsqueeze(1).to_broadcast([P, HEADS, ROPE_HALF])
                            st(ve.tensor_tensor(tm[q][:, t, :, :], a[:, t, :, :], tr, ALU.mult))
                    st(ve.tensor_tensor(x1, tm[0], tm[1], ALU.subtract))
                    st(ve.tensor_tensor(x2, tm[2], tm[3], ALU.add), S["tok_ready"])
            base += 24
            attend("mla")
            attend("fox")
            ve.wait_ge(S["gn2_in"], 16)
            st(ve.scalar_tensor_tensor(mod[:, 4, :], mod[:, 4, :], 1.0, mod[:, 0, :], ALU.add, ALU.mult))
            base += 8
            for half in range(2):
                hs = slice(half * 512, (half + 1) * 512)
                for t in range(NT):
                    ve.wait_ge(S["lin_evacuated"], base + half * NT + t + 1)
                    st(ve.tensor_tensor(x_tok[:, t, hs], x_tok[:, t, hs], mod[:, 2, hs], ALU.mult))
                    st(ve.tensor_tensor(x_tok[:, t, hs], x_tok[:, t, hs], h2_tok[:, t, hs], ALU.add), S["x2_ready"])
            for t in range(NT):
                ve.wait_ge(S["h2_std"], t + 1)
                st(ve.reciprocal(rstd[:, t:t + 1], rstd[:, t:t + 1]))
                st(ve.scalar_tensor_tensor(h2_tok[:, t, :], x_tok[:, t, :], rstd[:, t:t + 1], mod[:, 4, :], ALU.mult, ALU.mult))
                st(ve.tensor_tensor(h2_tok[:, t, :], h2_tok[:, t, :], mod[:, 3, :], ALU.add), S["h2_ready"])

            def top16(vals, n, v_out, i_out):
                st(ve.max(v_out[:, 0:8], vals))
                st(ve.max_index(i_out[:, 0:8], v_out[:, 0:8], vals))
                st(ve.match_replace(vals, v_out[:, 0:8], vals, -3.0e38))
                st(ve.max(v_out[:, 8:16], vals))
                st(ve.max_index(i_out[:, 8:16], v_out[:, 8:16], vals))

            def route(n):
                t, h = n // HEADS, n % HEADS
                ve.wait_ge(S["sc_copied"], n + 1)
                for p in range(2):
                    k = 2 * h + p
                    top16(scores[t % 2][:, k * P:(k + 1) * P], P, top_v[:, p * TOPK:(p + 1) * TOPK], top_i[:, p * TOPK:(p + 1) * TOPK])
                st(ve.tensor_copy(top_if[:, :], top_i[:, :]))
                c3 = cand.rearrange("p (i j) -> p i j", i=TOPK)
                st(ve.tensor_tensor(c3, top_v[:, 0:TOPK].unsqueeze(2).to_broadcast([P, TOPK, TOPK]),
                                    top_v[:, TOPK:].unsqueeze(1).to_broadcast([P, TOPK, TOPK]), ALU.add))
                top16(cand, 256, best_v[:, :], best_i[:, :])
                st(ve.tensor_scalar(best_hi[:, 0:TOPK], best_i[:, :], 4, None, ALU.logical_shift_right))
                st(ve.tensor_scalar(best_hi[:, TOPK:], best_i[:, :], 15, None, ALU.bitwise_and))
                st(ve.tensor_copy(best_f[:, :], best_hi[:, :]))
                oh = onehot[:, :].rearrange("p (k i) -> p k i", i=TOPK)
                st(ve.tensor_tensor(oh, best_f[:, :].unsqueeze(2).to_broadcast([P, 2 * TOPK, TOPK]),
                                    cst[:, CST["iota16"]].unsqueeze(1).to_broadcast([P, 2 * TOPK, TOPK]), ALU.is_equal))
                for p in range(2):
                    o = oh[:, p * TOPK:(p + 1) * TOPK, :]
                    st(ve.tensor_tensor(o, o, top_if[:, p * TOPK:(p + 1) * TOPK].unsqueeze(1).to_broadcast([P, TOPK, TOPK]), ALU.mult))
                st(ve.reduce_sum(e_f[:, :], oh, axis=AX_X))
                st(ve.scalar_tensor_tensor(e_f[:, 0:TOPK], e_f[:, 0:TOPK], float(N_KEYS), e_f[:, TOPK:], ALU.mult, ALU.add))
                st(ve.tensor_copy(idx[:, t, h * TOPK:(h + 1) * TOPK], e_f[:, 0:TOPK]))
                st(ve.tensor_scalar(gate_w[:, t % 2, h * TOPK:(h + 1) * TOPK], best_v[:, :], best_v[:, 0:1], None, ALU.subtract), S["top_arg"])
                ve.wait_ge(S["top_exp"], n + 1)
                st(ve.reciprocal(gsum[:, n % 2:n % 2 + 1], gsum[:, n % 2:n % 2 + 1]))
                g = gate_w[:, t % 2, h * TOPK:(h + 1) * TOPK]
                st(ve.tensor_scalar(g, g, gsum[:, n % 2:n % 2 + 1], None, ALU.mult))

            route(0)
            route(1)
            per_tile = ROWS_PER_TILE // UG

            def weigh(n):
                t, q = n // per_tile, n % per_tile
                ve.wait_ge(S["gl_ready"], n + 1)
                if n >= 2:
                    ve.wait_ge(S["dg_ready"], UG * (n - 1))
                st(ve.tensor_tensor(wts[:, n % 2, :], gl[:, n % 2, :], gate_w[:, t % 2, q * UG:(q + 1) * UG], ALU.mult), S["w_ready"])

            def finish(t):
                ve.wait_ge(S["v_used"], ROWS_PER_TILE * (t + 1))
                for half in range(2):
                    hs = slice(half * 512, (half + 1) * 512)
                    st(ve.tensor_tensor(h2_tok[:, t, hs], psum[(6, 0)[t % 2] + half][:, :], mod[:, 5, hs], ALU.mult))
                    st(ve.tensor_tensor(x_tok[:, t, hs], x_tok[:, t, hs], h2_tok[:, t, hs], ALU.add),
                       S["y_added"] if half else None)
            for t in range(NT):
                for q in range(per_tile):
                    n = t * per_tile + q
                    for s in range(UG):
                        slot = n % 2 * UG + s
                        ve.wait_ge(u_landed[slot], 16 * (n // 2 + 1))
                        if n >= 2 and s == 0:
                            ve.wait_ge(S["gl_ready"], n - 1)
                        st(ve.tensor_tensor_reduce(out=u_rows[:, slot, :], in0=u_rows[:, slot, :], in1=h2_tok[:, t, :], scale=1.0,
                                                   scalar=0.0, op0=ALU.mult, op1=ALU.add, accum_out=dots[:, n % 2, s:s + 1]), S["u_used"])
                    if n >= 1:
                        weigh(n - 1)
                    if n % PER_HEAD == 2 and n // PER_HEAD + 2 < NT * HEADS:
                        route(n // PER_HEAD + 2)
                    if t >= 1 and q == 4:
                        finish(t - 1)
            weigh(NT * per_tile - 1)
            finish(NT - 1)


def _chunks_fm(w, kb=KB):
    K, N = w.shape
    blocks = w.reshape(K // P, P, N // P, P).transpose(2, 1, 0, 3)
    blocks = blocks.reshape(N // P, P, K)
    if K <= CH:
        m = CH // K
        return blocks.reshape(N // P // m, m, P, K).transpose(0, 2, 1, 3).reshape(-1, P, CH)
    return blocks.reshape(N // P, P, K // CH, CH).transpose(0, 2, 1, 3).reshape(-1, P, CH)


def _chunks_tok(w, pad=0):
    K, N = w.shape
    per = CH // N
    if pad:
        a = w.reshape(K // P, P, N).transpose(1, 0, 2).reshape(1, P, K // P * N)
        return np.concatenate([a, np.zeros((1, P, CH - a.shape[2]), w.dtype)], axis=2)
    if N * (K // P) < CH or CH % N:
        a = w.reshape(K // P, P, N)
        return np.concatenate([a, np.zeros((K // P, P, CH - N), w.dtype)], axis=2) if N < CH else a
    return w.reshape(K // P // per, per, P, N).transpose(0, 2, 1, 3).reshape(-1, P, CH)


def lay_out(i):
    g = lambda n: np.asarray(i[n])
    x, w_in, w_in2 = g("x")[0], g("w_in")[0], g("w_in_2")
    col = lambda v: v.reshape(-1, P).T
    fm = lambda a: a.T.reshape(-1, P, a.shape[0]).transpose(1, 0, 2)
    q_cols = w_in[:, 0:512].reshape(D, 2, 4, 64).transpose(0, 2, 1, 3).reshape(D, 512)
    wkv = g("w_kv_mem")[0]
    gate = w_in[:, 2304:].reshape(D, 3, D)
    br = g("w_branch")[0]
    ukv = g("w_ukv_2").reshape(256, HEADS, 2, 64).transpose(0, 2, 1, 3).reshape(256, 1024)
    parts = [
        _chunks_tok(w_in[:, 640:768]), _chunks_fm(q_cols), _chunks_fm(w_in[:, 512:640]),
        _chunks_fm(wkv[:, 0:512]), _chunks_tok(wkv[:, 512:1024]),
        _chunks_tok(w_in[:, 1280:1792]), _chunks_fm(w_in[:, 768:1280]), _chunks_fm(w_in[:, 1792:2304])]
    for n in range(3):
        parts += [_chunks_fm(gate[:, n, :]), _chunks_fm(br[n])]
    parts += [_chunks_fm(g("w_out")[0]), _chunks_fm(g("w_q_mem")[0]), _chunks_fm(g("w_o_mem")[0]),
              _chunks_fm(g("w_up")[0]), _chunks_fm(g("w_down")[0]),
              _chunks_fm(w_in2[:, 0:640]),
              _chunks_tok(np.concatenate([w_in2[:, 640:672], w_in2[:, 2208:2216]], axis=1), pad=1),
              _chunks_tok(w_in2[:, 672:1184]), _chunks_tok(w_in2[:, 1184:1696]), _chunks_tok(w_in2[:, 1696:2208]),
              _chunks_tok(g("w_uq_2")), _chunks_tok(ukv),
              _chunks_tok(g("w_o_2")[:, 0:512]), _chunks_tok(g("w_o_2")[:, 512:1024]), _chunks_fm(g("w_pq_2"))]
    counts = [p.shape[0] for p in parts]
    want = [n for _, n in STREAM[:-2]] + [4, 4, 16]
    assert counts == want, (counts, want)
    gn = g("g_norm")[0]
    cols = np.concatenate([col(g("c_2")[0])] + [col(gn[k]) for k in range(6)] +
                          [col(g("g_mem")[0]), col(g("pool_scale")[0]), col(g("mla_qa_g_2")), col(g("mla_kva_g_2")),
                           col(g("norm1_g_2"))], axis=1)
    rows = np.concatenate([g("attn_sinks")[0], g("b_f_2"), g("mla_q_g_2"), g("mla_k_g_2"), g("fox_q_g_2"), g("fox_k_g_2")])[None]
    r, c = np.arange(P)[:, None], np.arange(256)[None]
    qc, kc = r // 64 + 2, c // 64
    band = np.where((kc <= qc) & (kc >= qc - 2), 0.0, NEG)
    diag = np.where(np.arange(P)[None] <= r, 0.0, NEG)
    inv_freq = (np.float32(10000.0) ** (-np.arange(0, 32, 2, dtype=np.float32) / np.float32(32))).astype(np.float32)
    cst = np.concatenate([np.eye(P), band, diag, np.tile(np.arange(16), (P, 1)), np.tile(inv_freq, (P, 1))], axis=1).astype(np.float32)
    t = np.arange(SEQ)
    inv_cnt = np.concatenate([1.0 / np.minimum(t + 1, w) for w in (2, 4, 8, 16)]).astype(np.float32)[None]
    sel = np.repeat(np.eye(HEADS), P, axis=1).astype(np.float32)
    c_ = np.ascontiguousarray
    return {
        "w_stream": c_(np.concatenate(parts, axis=0)), "xT": c_(fm(x)), "memT": c_(fm(g("mem")[0])), "cols": c_(cols),
        "rows": c_(rows), "cst": c_(cst), "inv_cnt": c_(inv_cnt), "sel": c_(sel),
        "sgu_rows": c_(np.concatenate([g("g_sgu")[0], g("b_spatial")[0].reshape(-1)])[None]),
        "w_pool": c_(g("w_pool")[0].transpose(1, 0, 2)), "w_spT": c_(g("w_spatial")[0].transpose(2, 0, 1)),
        "positions": c_(g("positions_2")[0].reshape(NT, P).T), "b_ada": c_(g("b_ada_2")[None]), "w_ada": c_(g("w_ada_2")),
        "norm2_g": c_(g("norm2_g_2")[None]),
        "sub_keys": c_(g("sub_keys_2").reshape(2 * HEADS, N_KEYS, P).transpose(2, 0, 1)),
        "peer_u": c_(g("peer_u_2")), "peer_v": c_(g("peer_v_2")),
    }


def kernel(**inputs):
    import concourse.bacc as bacc
    from concourse.bass_utils import run_bass_kernel_spmd

    nc = bacc.Bacc("TRN2", target_bir_lowering=False, num_devices=1)
    arrays = lay_out(inputs)
    T = {n: nc.dram_tensor("in_" + n, a.shape, mybir.dt.from_np(a.dtype), kind="ExternalInput").ap() for n, a in arrays.items()}
    out = nc.dram_tensor("out", (SEQ, D), F32, kind="ExternalOutput").ap()
    build(nc, T, out)
    r = run_bass_kernel_spmd(nc, [{"in_" + n: a for n, a in arrays.items()}], core_ids=[0])
    return np.asarray(r.results[0]["out"]).reshape(1, SEQ, D)
```

```python
import math
from contextlib import ExitStack

import numpy as np
import concourse.bass as bass
from concourse import mybir

F32 = mybir.dt.float32
U32 = mybir.dt.uint32
I32 = mybir.dt.int32
ALU = mybir.AluOpType
ACT = mybir.ActivationFunctionType
AX_X = mybir.AxisListType.X
ds = bass.ds

P = 128
SEQ = 512
NT = SEQ // P
D = 1024
KB = D // P
N_MEM = 256
EPS = 1e-6
FAR = 1e30
FF_BLOCKS = 32
CH = 1024
RING = 4
TOPK = 16
HEADS = 8
N_KEYS = 128
QK = 96
ROPE_HALF = 16
POOL_PAD = 16
UG = 4
ROWS_PER_TILE = HEADS * TOPK
PER_HEAD = TOPK // UG
AHEAD = 14
W_RING = 24
QUERY_GROUPS = 2 * (HEADS - 1)

COLS = {}
_at = 0
for _name, _n in (("c", 8), ("g0", 8), ("g1", 8), ("g2", 8), ("g3", 8), ("g4", 8), ("g5", 8),
                  ("g_mem", 8), ("pool_scale", 4), ("qa_g", 3), ("kva_g", 2), ("norm1_g", 8)):
    COLS[_name] = slice(_at, _at + _n)
    _at += _n
N_COLS = _at
ROWS = {}
_at = 0
for _name, _n in (("sinks", 8), ("b_f", 8), ("mla_q_g", QK), ("mla_k_g", QK), ("fox_q_g", 64), ("fox_k_g", 64)):
    ROWS[_name] = slice(_at, _at + _n)
    _at += _n
N_ROWS = _at
CST = {"ident": slice(0, 128), "mask_band": slice(128, 384), "mask_causal": slice(384, 896),
       "iota16": slice(896, 912), "inv_freq": slice(912, 928)}
N_CST = 928

STREAM = (("sgu_v", 4), ("pool_c", 4), ("sgu_u", 4), ("kv_mem_k", 4), ("kv_mem_v", 4), ("v_attn", 1), ("q_attn", 4), ("k_attn", 1), ("gate0", 8), ("branch0", 4), ("gate1", 8), ("branch1", 4), ("gate2", 8), ("branch2", 4),
          ("out", 8), ("q_mem", 4), ("o_mem", 4), ("up", 32), ("down", 32),
          ("cq_ckv", 5), ("misc", 1), ("fox_q", 4), ("fox_k", 4), ("fox_v", 4), ("ukv", 2), ("uq", 3), ("o2", 8), ("pq", 16))
N_CHUNKS = sum(n for _, n in STREAM)
LIN_MOD_COLS = 27 + 8 + 48 + 8 + 4 + 8 + 32 + 8 + 1

MAGIC = 12582912.0
TWO_PI_A = 6.28125
TWO_PI_B = 0.0019350051879882812
TWO_PI_C = 2 * math.pi - TWO_PI_A - TWO_PI_B


class Steps:

    def __init__(self, eng, own):
        self.eng, self.own, self.count, self.loop = eng, own, {}, None

    def value(self, sem):
        n = self.count.get(sem.name, 0)
        if self.loop is not None and sem.name in self.loop[1]:
            reg, per, base = self.loop
            return reg * per[sem.name] + n
        return n

    def tell(self, ins, sem, by=1):
        self.count[sem.name] = self.count.get(sem.name, 0) + by
        ins.then_inc(sem, by)

    def __call__(self, ins, sem=None):
        sem = self.own if sem is None else sem
        self.tell(ins, sem)
        self.eng.wait_ge(sem, self.value(sem))

    def enter(self, reg, per):
        self.loop = (reg, {s.name: k for s, k in per}, dict(self.count))

    def leave(self, iterations):
        _, per, base = self.loop
        for name, k in per.items():
            assert self.count[name] - base.get(name, 0) == k, (name, self.count[name], base.get(name, 0), k)
            self.count[name] = base.get(name, 0) + k * iterations
        self.loop = None


def attention_plan():
    plan = {}
    u = g = 0
    for kind, heads in (("band", 8), ("mem", 4), ("mla", 8), ("fox", 8)):
        units = []
        for t in range(NT):
            for h in range(heads):
                if kind == "band":
                    blocks = [t - 1, t] if t else [0]
                elif kind == "mem":
                    blocks = [0, 1]
                else:
                    blocks = list(range(t + 1))
                units.append(dict(u=u, g=g, t=t, h=h, blocks=blocks, last=h == heads - 1))
                u += 1
            g += 1
        plan[kind] = dict(units=units, heads=heads, dv=512 // heads)
    return plan


def build(nc, T, out):
    plan = attention_plan()
    with ExitStack() as ctx:
        def sb(name, shape, dt=F32):
            return ctx.enter_context(nc.sbuf_tensor(name, shape, dt))

        def sem(name):
            return ctx.enter_context(nc.semaphore(name))

        main = sb("main", [P, 4 * 4096 + 20480])
        def region(lo, *shape):
            n = int(np.prod(shape))
            v = main[:, lo:lo + n]
            if len(shape) == 2:
                return v.rearrange("p (a b) -> p a b", a=shape[0])
            if len(shape) == 3:
                return v.rearrange("p (a b c) -> p a b c", a=shape[0], b=shape[1])
            return v
        X0, H0, Z0, S0, A0 = 0, 4096, 8192, 12288, 16384
        xT = region(X0, KB, SEQ)
        hT = region(H0, KB, SEQ)
        zT = region(Z0, KB, SEQ)
        sqT = region(S0, KB, SEQ)
        inv_cnt = region(Z0, 4, SEQ)
        g_sgu_row = region(Z0 + 2048, 512)
        b_sp_row = region(Z0 + 2560, 4, P)
        w_pool = region(Z0 + 3072, 4, P)
        w_spT = region(Z0 + 3584, 4, P)
        uT = region(A0, 4, SEQ)
        cT = region(A0 + 2048, 4, SEQ + POOL_PAD)
        yaT = region(A0 + 4160, 4, SEQ)
        kmT = region(A0 + 6208, 4, N_MEM)
        vm = region(A0 + 7232, 2, 512)
        q1T = region(A0 + 8256, 4, SEQ)
        k1T = region(A0 + 10304, SEQ)
        v1 = region(A0 + 10816, NT, P)
        vS = region(A0 + 11328, NT, 512)
        memT = region(A0 + 13376, KB, N_MEM)
        gates = region(A0 + 8256, KB, SEQ)
        merged = region(A0 + 12352, KB, SEQ)
        pool_a = region(A0 + 16448, SEQ + POOL_PAD)
        pool_b = region(A0 + 16976, SEQ + POOL_PAD)
        ycT = region(A0 + 17504, 4, SEQ)
        qmT = region(A0 + 8256, 4, SEQ)
        ymT = region(A0 + 10304, 4, SEQ)
        hid = region(A0, FF_BLOCKS, SEQ)
        probs = region(S0, 3, 512)
        probsT = region(S0 + 1536, 2, 512)
        o_tok = region(S0 + 2560, 2, 512)
        qT = region(A0, HEADS, SEQ)
        kT = region(A0 + 4096, HEADS, SEQ)
        k_tok = region(A0, NT, HEADS, QK)
        q_tok = region(H0, NT, HEADS, QK)
        cqT = region(A0 + 4096, 5, SEQ)
        fqT = region(A0 + 8192, 4, SEQ)
        fkT = region(A0 + 10240, 4, SEQ)
        f_row = region(A0 + 12288, HEADS, SEQ)
        v_mla = region(A0 + 16384, NT, 512)
        v_fox = region(A0 + 18432, NT, 512)
        fq_tok = region(Z0, NT, 512)
        fk_tok = region(Z0 + 2048, NT, 512)
        sq_tok = region(S0, NT, HEADS * QK)
        rope_tmp = region(S0 + 3072, 1024)
        oT = region(H0, KB, SEQ)
        u_rows = region(A0, 2 * UG, D)
        v_rows = region(A0 + 8192, 2 * UG, D)
        x_tok = region(A0 + 16384, NT, D)
        h2_tok = region(S0, NT, D)
        h2T = region(Z0, KB, SEQ)
        qpT = region(X0, 2 * HEADS, SEQ)

        ring = sb("ring", [P, RING, CH])
        ada_ring = sb("ada_ring", [P, 2, CH])
        sub_keys = ada_ring[:, :, :].rearrange("p a b -> p (a b)").rearrange("p (k n) -> p k n", n=N_KEYS)
        mod = sb("mod", [P, 6, D])
        scores = [mod[:, 0:2, :].rearrange("p a b -> p (a b)"), ring[:, 0:2, :].rearrange("p a b -> p (a b)")]
        onehot = sb("onehot", [P, 2 * TOPK * TOPK])
        cols = sb("cols", [P, N_COLS])
        rows = sb("rows", [P, N_ROWS])
        cst = sb("cst", [P, N_CST])
        sel = mod[0:HEADS, 1, :]
        ones = sb("ones", [P, P])
        diag = sb("diag", [P, NT, P])
        eps = sb("eps", [P, 1])
        std = sb("std", [P, NT])
        rstd = sb("rstd", [P, NT])
        silu_c = sb("silu_c", [P, KB])
        c_now = sb("c_now", [P, 1])
        mx = sb("mx", [P, 2, HEADS])
        neg_m = sb("neg_m", [P, 2, HEADS])
        row_sum = sb("row_sum", [P, 2, HEADS])
        sink_e = sb("sink_e", [P, 2, HEADS])
        ident = cst[:, CST["ident"]]
        cand = cst[:, CST["mask_band"]]
        small = sb("small", [P, 580])

        def sm(lo, n):
            return small[:, lo:lo + n]
        mod_cols = sm(484, 2 * KB)
        misc_tok = sm(0, 160).rearrange("p (t n) -> p t n", t=NT)
        fl_a = sm(160, 32)
        fl_b = sm(192, 32)
        pos_f = sm(224, 4)
        ang = sm(228, 64)
        turns = sm(292, 64)
        sin_t = sm(356, 64)
        cos_t = sm(420, 64)
        ss_tok = sm(484, 32)
        r_tok = sm(516, 32)
        fq_col = sm(548, 32).rearrange("p (t h) -> p t h", t=NT)
        pos_i = sb("pos_i", [P, NT], I32)
        f_cum = diag[0:HEADS, :, :].rearrange("p a b -> p (a b)")
        f_log = mod[0:HEADS, 0, 0:512]

        psum = [ctx.enter_context(nc.psum_tensor(f"bank{i}", [P, 512], F32)) for i in range(8)]

        names = ("consts_in cols_in rows_in x_in mem_in sgu_in ada_b_in pos_in sub_in sel_in gn2_in "
                 "w_used lin_ready lin_evacuated sq_ready sumsq_ready std_ready diag_ready rbc_ready h_ready mem_ready "
                 "ones_ready acc_zero sig_c x_ready silu_ready v_sq_ready vstd_ready vs_ready wsp_ready yb_ready pooled_ready "
                 "merged_ready hid_ready ada_used cqn_ready "
                 "s_ready neg_ready p_ready pt_ready pt_copied av_done o_normed ot_ready ot_copied sink_arg sink_exp "
                 "fl_arg fl_exp fl_ready f_cum_ready trig_arg trig_ready tok_sq tok_ss tok_std tok_ready "
                 "h2_sq h2_std h2_ready x2_ready sc_ready sc_copied top_arg top_exp "
                 "u_used gl_ready w_ready dg_ready v_used y_added stored "
                 "dve_own").split()
        S = {n: sem(n) for n in names}
        w_landed = [sem(f"w_landed{i}") for i in range(RING)]
        ada_landed = [sem(f"ada_landed{i}") for i in range(2)]
        u_landed = [sem(f"u_landed{i}") for i in range(2 * UG)]
        v_landed = [sem(f"v_landed{i}") for i in range(2 * UG)]
        idx = sb("idx", [P, NT, ROWS_PER_TILE], U32)
        gate_w = sb("gate_w", [P, 2, ROWS_PER_TILE])
        top_v = sm(0, 2 * TOPK)
        top_i = sb("top_i", [P, 2 * TOPK], U32)
        top_if = sm(32, 2 * TOPK)
        best_v = sm(64, TOPK)
        best_i = sb("best_i", [P, TOPK], U32)
        best_hi = sb("best_hi", [P, 2 * TOPK], U32)
        best_f = sm(80, 2 * TOPK)
        e_f = sm(112, 2 * TOPK)
        gsum = sm(144, 2)
        dots = sm(146, 2 * UG).rearrange("p (a b) -> p a b", a=2)
        gl = sm(154, 2 * UG).rearrange("p (a b) -> p a b", a=2)
        wts = sm(162, W_RING * UG).rearrange("p (a b) -> p a b", a=W_RING)
        wdiag = diag

        block = ctx.enter_context(nc.Block())

        @block.sync
        def _(sp):
            w = T["w_stream"]
            sp.dma_start(cols[:, :], T["cols"]).then_inc(S["cols_in"], 16)
            for s in range(RING):
                sp.dma_start(ring[:, s, :], w[s]).then_inc(w_landed[s], 16)
            n = N_CHUNKS // RING
            with sp.Fori(1, n) as i:
                for s in range(RING):
                    sp.wait_ge(S["w_used"], i * RING + (s - RING + 1))
                    sp.dma_start(ring[:, s, :], w[ds(i * RING + s, 1)].rearrange("a p n -> p (a n)")).then_inc(w_landed[s], 16)
            for c in range(n * RING, N_CHUNKS):
                sp.wait_ge(S["w_used"], c - RING + 1)
                sp.dma_start(ring[:, c % RING, :], w[c]).then_inc(w_landed[c % RING], 16)
            for t in range(NT):
                sp.wait_ge(S["y_added"], t + 1)
                sp.dma_start(out[t * P:(t + 1) * P, :], x_tok[:, t, :]).then_inc(S["stored"], 16)
            sp.wait_ge(S["stored"], 16 * NT)

        @block.gpsimd
        def _(gp):
            gp.memset(ones[:, :], 1.0).then_inc(S["ones_ready"], 1)
            gp.memset(eps[:, :], EPS).then_inc(S["ones_ready"], 1)
            gp.memset(mod[:, :, :].rearrange("p a b -> p (a b)"), 0.0).then_inc(S["acc_zero"], 1)
            gp.dma_start(memT, T["memT"]).then_inc(S["mem_in"], 16)
            gp.dma_start(inv_cnt, T["inv_cnt"].to_broadcast([P, 4 * SEQ]).rearrange("p (a b) -> p a b", a=4)).then_inc(S["sgu_in"], 16)
            gp.dma_start(region(Z0 + 2048, 1024), T["sgu_rows"].to_broadcast([P, 1024])).then_inc(S["sgu_in"], 16)
            gp.dma_start(w_pool, T["w_pool"]).then_inc(S["sgu_in"], 16)
            gp.dma_start(w_spT, T["w_spT"]).then_inc(S["sgu_in"], 16)
            gp.dma_start(rows[:, :], T["rows"].to_broadcast([P, N_ROWS])).then_inc(S["rows_in"], 16)
            gp.dma_start(pos_i[:, :], T["positions"]).then_inc(S["pos_in"], 16)
            gp.wait_ge(S["acc_zero"], 1)
            gp.dma_start(mod[0:1, :, :].rearrange("p a b -> p (a b)"), T["b_ada"]).then_inc(S["ada_b_in"], 16)
            for p in range(48):
                if p >= 2:
                    gp.wait_ge(S["ada_used"], p - 1)
                k, s = p // 6, p % 6
                gp.dma_start(ada_ring[:, p % 2, :], T["w_ada"][k * P:(k + 1) * P, s * D:(s + 1) * D]).then_inc(ada_landed[p % 2], 16)
            gp.wait_ge(S["ada_used"], 48)
            gp.dma_start(sub_keys, T["sub_keys"]).then_inc(S["sub_in"], 16)
            gp.wait_ge(S["lin_evacuated"], LIN_MOD_COLS)
            gp.dma_start(sel, T["sel"]).then_inc(S["sel_in"], 16)
            gp.wait_ge(S["f_cum_ready"], 1)
            gp.dma_start(mod[:, 0, :], T["norm2_g"].to_broadcast([P, D])).then_inc(S["gn2_in"], 16)

            def gather(rows_buf, table, slot, t, j, landed):
                gp.indirect_dma_start(rows_buf[:, slot, :], None, table,
                                      bass.IndirectOffsetOnAxis(ap=idx[:, t, j:j + 1], axis=0)).then_inc(landed[slot], 16)
            n_groups = NT * ROWS_PER_TILE // UG
            per_tile = ROWS_PER_TILE // UG
            for g in range(n_groups + AHEAD + 1):
                if g < n_groups:
                    t, j0 = g // per_tile, g % per_tile * UG
                    if g % PER_HEAD == 0:
                        gp.wait_ge(S["top_arg"], g // PER_HEAD + 1)
                        if g == 0:
                            gp.wait_ge(S["x2_ready"], 2 * NT)
                    for s in range(UG):
                        if g >= 2:
                            gp.wait_ge(S["u_used"], UG * (g - 2) + s + 1)
                        gather(u_rows, T["peer_u"], g % 2 * UG + s, t, j0 + s, u_landed)
                q = g - (AHEAD + 1)
                if q >= 0:
                    t, j0 = q // per_tile, q % per_tile * UG
                    for s in range(UG):
                        if q >= 2:
                            gp.wait_ge(S["v_used"], UG * (q - 2) + s + 1)
                        gather(v_rows, T["peer_v"], q % 2 * UG + s, t, j0 + s, v_landed)

        @block.tensor
        def _(pe):
            chunk = [0]
            release = [0]
            lin = [0]
            loop = [None]

            mm = pe.matmul

            def mmw(o, lhsT, rhs, **kw):
                ins = pe.matmul(o, lhsT, rhs, **kw)
                if release[0]:
                    ins.then_inc(S["w_used"], release[0])
                    release[0] = 0
                return ins

            def take():
                c = chunk[0]
                chunk[0] += 1
                v = 16 * (c // RING + 1)
                if loop[0] is not None:
                    v = loop[0][0] * (16 * (loop[0][1] // RING)) + v
                pe.wait_ge(w_landed[c % RING], v)
                return ring[:, c % RING, :]

            def bank():
                n = lin[0] - 3
                if loop[0] is not None:
                    pe.wait_ge(S["lin_evacuated"], loop[0][0] * loop[0][2] + n)
                elif n > 0:
                    pe.wait_ge(S["lin_evacuated"], n)
                lin[0] += 1
                return psum[(lin[0] - 1) % 4]

            def results(ins, n=1):
                ins.then_inc(S["lin_ready"], n)

            def loops(n, chunks, outs, body):
                assert chunks % RING == 0 and outs % 4 == 0 and lin[0] >= 4 and release[0] == 1
                c0, l0 = chunk[0], lin[0]
                with pe.Fori(0, n) as i:
                    loop[0] = (i, chunks, outs)
                    body()
                    loop[0] = None
                assert chunk[0] == c0 + chunks and lin[0] == l0 + outs and release[0] == 1
                chunk[0], lin[0] = c0 + n * chunks, l0 + n * outs

            def linear_fm(src, n_chunks, kb=KB, width=SEQ, first_wait=None):
                for c in range(n_chunks):
                    w = take()
                    for m in range(KB // kb):
                        b = bank()
                        for k in range(kb):
                            if first_wait is not None and c == 0 and m == 0:
                                first_wait(k)
                            last = mmw(b[:, 0:width], w[:, (m * kb + k) * P:(m * kb + k + 1) * P], src[:, k, 0:width],
                                      start=k == 0, stop=k == kb - 1)
                        results(last)
                    release[0] += 1

            def linear_tok(src, n_chunks, width, tiles=NT, kb=KB, first_wait=None):
                banks = [bank() for _ in range(tiles)]
                for c in range(n_chunks):
                    w = take()
                    for kk in range(kb // n_chunks):
                        k = c * (kb // n_chunks) + kk
                        if first_wait is not None:
                            first_wait(k)
                        for t in range(tiles):
                            last = mmw(banks[t][:, 0:width], src[:, k, t * P:(t + 1) * P], w[:, kk * width:(kk + 1) * width],
                                      start=k == 0, stop=k == kb - 1)
                    release[0] += 1
                results(last, tiles)

            norms = [0]
            sq_seen = [0]

            def norm(nb, tiles=NT, first=0):
                for k in range(nb):
                    sq_seen[0] += 1
                    pe.wait_ge(S["sq_ready"], sq_seen[0])
                    for t in range(tiles):
                        last = mm(psum[6][:, t:t + 1], sqT[:, first + k, t * P:(t + 1) * P], ones[:, 0:1],
                                  start=k == 0 and t == 0, stop=k == nb - 1, skip_group_check=True)
                last.then_inc(S["sumsq_ready"], 1)
                norms[0] += 1
                pe.wait_ge(S["diag_ready"], norms[0])
                mm(psum[7][:, 0:tiles * P], ones[:, :], diag[:, 0:tiles, :], start=True, stop=True).then_inc(S["rbc_ready"], 1)

            h_seen = [0]

            def h_block(k):
                pe.wait_ge(S["h_ready"], h_seen[0] + k + 1)

            def attend(kind, q_of, k_of, v_of):
                units, dv = plan[kind]["units"], plan[kind]["dv"]
                n = len(units)
                pe.wait_ge(S["lin_evacuated"], lin[0])
                tile_end = {}
                for i in range(n + 6):
                    if i < n:
                        x = units[i]
                        u = x["u"]
                        if u >= 3:
                            pe.wait_ge(S["p_ready"], u - 2)
                        b0, nk = x["blocks"][0], len(x["blocks"]) * P
                        mm(psum[3 + u % 3][:, 0:nk], q_of(x), k_of(x, b0 * P, nk), start=True, stop=True).then_inc(S["s_ready"], 1)
                    if 2 <= i <= n + 1:
                        x = units[i - 2]
                        u = x["u"]
                        pe.wait_ge(S["p_ready"], u + 1)
                        if u >= 2:
                            pe.wait_ge(S["pt_copied"], u - 1)
                        for j in range(len(x["blocks"])):
                            last = pe.transpose(psum[6 + u % 2][:, j * P:(j + 1) * P], probs[:, u % 3, j * P:(j + 1) * P], ident)
                        last.then_inc(S["pt_ready"], 1)
                    if 3 <= i <= n + 2:
                        x = units[i - 3]
                        u, g = x["u"], x["g"]
                        pe.wait_ge(S["pt_copied"], u + 1)
                        if x["h"] == 0 and g >= 2:
                            pe.wait_ge(S["o_normed"], g - 1)
                        for j, kb_ in enumerate(x["blocks"]):
                            last = mm(psum[g % 2][:, x["h"] * dv:(x["h"] + 1) * dv], probsT[:, u % 2, j * P:(j + 1) * P],
                                      v_of(x, kb_), start=j == 0, stop=j == len(x["blocks"]) - 1)
                        last.then_inc(S["av_done"], 1)
                        if x["last"]:
                            tile_end[i + 2] = g
                    if i in tile_end:
                        g = tile_end[i]
                        pe.wait_ge(S["o_normed"], g + 1)
                        if g >= 1:
                            pe.wait_ge(S["ot_copied"], g)
                        for j in range(4):
                            last = pe.transpose(psum[2][:, j * P:(j + 1) * P], o_tok[:, g % 2, j * P:(j + 1) * P], ident)
                        last.then_inc(S["ot_ready"], 1)
                assert len(tile_end) == NT
                pe.wait_ge(S["ot_copied"], units[-1]["g"] + 1)

            pe.wait_ge(S["consts_in"], 16)
            pe.wait_ge(S["ones_ready"], 2)
            norm(KB)
            norm(KB, tiles=2)
            linear_tok(hT, 4, 512, first_wait=h_block)
            linear_fm(hT, 8)
            pe.wait_ge(S["mem_ready"], KB)
            linear_fm(memT, 4, width=N_MEM)
            linear_tok(memT, 4, 512, tiles=2)
            linear_tok(hT, 1, P)
            linear_fm(hT, 5)
            h_seen[0] += KB
            attend("band",
                   lambda x: q1T[x["h"] // 4 * 64:x["h"] // 4 * 64 + 64, x["h"] % 4, x["t"] * P:(x["t"] + 1) * P],
                   lambda x, k0, nk: k1T[x["h"] // 4 * 64:x["h"] // 4 * 64 + 64, k0:k0 + nk],
                   lambda x, b: v1[:, b, x["h"] // 4 * 64:x["h"] // 4 * 64 + 64])
            pe.wait_ge(S["vs_ready"], NT)
            pe.wait_ge(S["wsp_ready"], 1)
            for g in range(4):
                b = bank()
                for t in range(NT):
                    last = mm(b[:, t * P:(t + 1) * P], vS[:, t, g * P:(g + 1) * P], w_spT[:, g, :], start=True, stop=True)
                results(last)
            pe.wait_ge(S["pooled_ready"], 4)
            for g in range(4):
                b = bank()
                results(mm(b[:, :], w_pool[:, g, :], cT[:, g, POOL_PAD:], start=True, stop=True))
            ybT = uT
            for n, y in enumerate((yaT, ybT, ycT)):
                loops(2, 4, 4, lambda: linear_fm(hT, 4))
                if n == 1:
                    pe.wait_ge(S["yb_ready"], 4)
                if n == 2:
                    pe.wait_ge(S["lin_evacuated"], lin[0])
                linear_fm(y, 4, kb=4)
            pe.wait_ge(S["merged_ready"], 3 * KB)
            loops(2, 4, 4, lambda: linear_fm(merged, 4))
            norm(KB)
            norm(KB)
            linear_fm(hT, 4, first_wait=h_block)
            h_seen[0] += KB
            attend("mem",
                   lambda x: qmT[:, x["h"], x["t"] * P:(x["t"] + 1) * P],
                   lambda x, k0, nk: kmT[:, x["h"], 0:nk],
                   lambda x, b: vm[:, b, x["h"] * P:(x["h"] + 1) * P])
            linear_fm(ymT, 4, kb=4)
            norm(KB)
            norm(KB)
            for k in range(KB):
                h_block(k)
            h_seen[0] += KB
            loops(8, 4, 4, lambda: linear_fm(hT, 4))
            pe.wait_ge(S["hid_ready"], FF_BLOCKS)

            def down():
                for m in range(4):
                    b = bank()
                    for q in range(4):
                        w = take()
                        for k in range(KB):
                            last = mmw(b[:, :], w[:, k * P:(k + 1) * P], hid[:, q * KB + k, :],
                                      start=q == 0 and k == 0, stop=q == 3 and k == KB - 1)
                        release[0] += 1
                    results(last)
            loops(2, 16, 4, down)
            norm(KB)
            pe.wait_ge(S["ada_used"], 48)
            b = bank()
            for j in range(2 * KB):
                last = mm(b[:, j:j + 1], mod[:, 0:2, :].rearrange("p a b -> p (a b)")[:, j * P:(j + 1) * P], ones[:, 0:1],
                          start=True, stop=True)
            results(last)
            for s in range(2, 6):
                for half in range(2):
                    b = bank()
                    results(mm(b[:, :], ones[:, :], mod[:, s, half * 512:(half + 1) * 512], start=True, stop=True))
            norm(KB)
            linear_fm(hT, 5, first_wait=h_block)
            linear_tok(hT, 1, 40)
            linear_tok(hT, 4, 512)
            norm(3)
            norm(2, first=3)
            linear_tok(hT, 4, 512)
            linear_tok(hT, 4, 512)
            h_seen[0] += KB
            pe.wait_ge(S["cqn_ready"], 5)

            def linear_latent(first, nb, width):
                ws = []
                for half in range(2):
                    banks = [bank() for _ in range(NT)]
                    for k in range(nb):
                        if half == 0:
                            ws.append(take())
                        for t in range(NT):
                            last = mmw(banks[t][:, 0:width], cqT[:, first + k, t * P:(t + 1) * P],
                                       ws[k][:, half * width:(half + 1) * width], start=k == 0, stop=k == nb - 1)
                    results(last, NT)
                release[0] += nb
            linear_latent(3, 2, 512)
            linear_latent(0, 3, 384)
            pe.wait_ge(S["fl_ready"], 1)
            b = bank()
            for t in range(NT):
                last = pe.transpose(b[0:HEADS, t * P:(t + 1) * P], fl_a[:, t * HEADS:(t + 1) * HEADS], ident)
            results(last)
            for n, src in enumerate((fq_tok, fk_tok)):
                pe.wait_ge(S["tok_ready"], n + 1)
                for j in range(4):
                    b = bank()
                    for t in range(NT):
                        last = pe.transpose(b[:, t * P:(t + 1) * P], src[:, t, j * P:(j + 1) * P], ident)
                    results(last)

            def latent_heads(src):
                for h in range(HEADS):
                    b = bank()
                    for t in range(NT):
                        last = pe.transpose(b[0:QK, t * P:(t + 1) * P], src[:, t, h, :], ident)
                    results(last)
            pe.wait_ge(S["tok_ready"], 3)
            latent_heads(k_tok)
            pe.wait_ge(S["f_cum_ready"], 1)
            b = bank()
            for t in range(NT):
                last = pe.transpose(b[:, t * HEADS:(t + 1) * HEADS], f_cum[:, t * P:(t + 1) * P], ident[0:HEADS, 0:HEADS])
            results(last)
            pe.wait_ge(S["sel_in"], 16)
            for h in range(HEADS):
                b = bank()
                results(mm(b[:, :], sel[:, h * P:(h + 1) * P], f_cum, start=True, stop=True))
            pe.wait_ge(S["tok_ready"], 4)
            latent_heads(q_tok)
            attend("mla",
                   lambda x: qT[0:QK, x["h"], x["t"] * P:(x["t"] + 1) * P],
                   lambda x, k0, nk: kT[0:QK, x["h"], k0:k0 + nk],
                   lambda x, b: v_mla[:, b, x["h"] * 64:(x["h"] + 1) * 64])
            attend("fox",
                   lambda x: fqT[x["h"] % 2 * 64:x["h"] % 2 * 64 + 64, x["h"] // 2, x["t"] * P:(x["t"] + 1) * P],
                   lambda x, k0, nk: fkT[x["h"] % 2 * 64:x["h"] % 2 * 64 + 64, x["h"] // 2, k0:k0 + nk],
                   lambda x, b: v_fox[:, b, x["h"] * 64:(x["h"] + 1) * 64])
            for t in range(NT):
                for half in range(2):
                    b = bank()
                    for j in range(4):
                        last = pe.transpose(b[:, j * P:(j + 1) * P], xT[:, half * 4 + j, t * P:(t + 1) * P], ident)
                    results(last)
            linear_tok(oT, 4, 512)
            linear_tok(oT, 4, 512)
            for t in range(NT):
                pe.wait_ge(S["h2_ready"], t + 1)
                for half in range(2):
                    b = bank()
                    for j in range(4):
                        last = pe.transpose(b[:, j * P:(j + 1) * P], h2_tok[:, t, (half * 4 + j) * P:(half * 4 + j + 1) * P], ident)
                    results(last)
            pe.wait_ge(S["lin_evacuated"], lin[0])
            pe.wait_ge(S["sub_in"], 16)

            def key_scores(n):
                t, h = n // HEADS, n % HEADS
                if n >= 2:
                    pe.wait_ge(S["sc_copied"], n - 1)
                for p in range(2):
                    last = mm(psum[4 + n % 2][:, p * P:(p + 1) * P], qpT[:, 2 * h + p, t * P:(t + 1) * P],
                              sub_keys[:, 2 * h + p, :], start=True, stop=True)
                last.then_inc(S["sc_ready"], 1)

            def group(t, reg, q, first=False, last_group=False):
                y = [psum[(6, 0)[t % 2] + half] for half in range(2)]
                for s in range(UG):
                    n = t * per_tile + q
                    v = 16 * (n // 2 + 1)
                    dg = n * UG + s + 1
                    if reg is not None:
                        v = reg * 16 + v
                        dg = reg * (2 * UG) + dg
                    pe.wait_ge(v_landed[q % 2 * UG + s], v)
                    pe.wait_ge(S["dg_ready"], dg)
                    for half in range(2):
                        ins = mm(y[half][:, :], wdiag[:, s, :], v_rows[:, q % 2 * UG + s, half * 512:(half + 1) * 512],
                                 start=first and s == 0, stop=last_group and s == UG - 1)
                    ins.then_inc(S["v_used"], 1)
            per_tile = ROWS_PER_TILE // UG

            for h in range(HEADS):
                linear_fm(h2T, 2)
                pe.wait_ge(S["lin_evacuated"], lin[0])
                key_scores(h)
            for t in range(NT):
                if t + 1 < NT:
                    for h in range(HEADS):
                        key_scores(HEADS * (t + 1) + h)
                if t >= 2:
                    pe.wait_ge(S["y_added"], t - 1)
                group(t, None, 0, first=True)
                group(t, None, 1)
                with pe.Fori(0, per_tile // 2 - 2) as i:
                    group(t, i, 2)
                    group(t, i, 3)
                group(t, None, per_tile - 2)
                group(t, None, per_tile - 1, last_group=True)

        @block.scalar
        def _(ac):
            lin = [0]
            loop = [None]

            def ready(n=1):
                lin[0] += n
                v = lin[0]
                if loop[0] is not None:
                    v = loop[0][0] * loop[0][1] + v
                ac.wait_ge(S["lin_ready"], v)
                return psum[(lin[0] - 1) % 4]

            def evac(dst, func=ACT.Copy, width=512, rows_=P, src=None, **kw):
                b = ready()
                s = b[0:rows_, 0:width] if src is None else src(b)
                ac.activation(dst, s, func, **kw).then_inc(S["lin_evacuated"], 1)

            def squares(src_of, nb, width=SEQ, wait=None):
                for k in range(nb):
                    if wait is not None:
                        wait(k)
                    ac.activation(sqT[:, k, 0:width], src_of(k), ACT.Square).then_inc(S["sq_ready"], 1)

            norms = [0]

            def norm_std(width, tiles=NT):
                norms[0] += 1
                ac.wait_ge(S["sumsq_ready"], norms[0])
                ac.activation(std[:, 0:tiles], psum[6][:, 0:tiles], ACT.Sqrt, scale=1.0 / width, bias=eps[:, 0:1])\
                  .then_inc(S["std_ready"], 1)

            ac.dma_start(xT, T["xT"]).then_inc(S["x_in"], 16)
            ac.dma_start(cst[:, :], T["cst"]).then_inc(S["consts_in"], 16)
            ac.wait_ge(S["x_in"], 16)
            squares(lambda k: xT[:, k, :], KB)
            ac.wait_ge(S["ones_ready"], 2)
            norm_std(D)
            ac.wait_ge(S["mem_in"], 16)
            squares(lambda k: memT[:, k, :], KB, width=N_MEM)
            norm_std(D, tiles=2)
            ac.wait_ge(S["cols_in"], 16)
            ac.activation(silu_c[:, :], cols[:, COLS["c"]], ACT.Sigmoid).then_inc(S["sig_c"], 1)
            for t in range(NT):
                evac(vS[:, t, :], ACT.Gelu_apprx_tanh)
            for j in range(4):
                evac(cT[:, j, POOL_PAD:])
            for j in range(4):
                evac(uT[:, j, :], ACT.Gelu_apprx_tanh)
            ac.wait_ge(S["v_sq_ready"], NT)
            ac.activation(std[:, :], rstd[:, :], ACT.Sqrt, scale=1.0 / 512, bias=eps[:, 0:1]).then_inc(S["vstd_ready"], 1)
            for j in range(4):
                evac(kmT[:, j, :], width=N_MEM)
            for j in range(2):
                evac(vm[:, j, :])
            for t in range(NT):
                evac(v1[:, t, :], width=P)
            for j in range(4):
                evac(q1T[:, j, :], scale=-0.125)
            evac(k1T)

            def attend(kind, dst):
                units, heads = plan[kind]["units"], plan[kind]["heads"]
                n = len(units)
                tile_end = {}
                for i in range(n + 6):
                    if i < n:
                        x = units[i]
                        u, pr = x["u"], x["g"] % 2
                        nk = len(x["blocks"]) * P
                        ac.wait_ge(S["neg_ready"], u + 1)
                        if u >= 3:
                            ac.wait_ge(S["pt_ready"], u - 2)
                        ac.activation(probs[:, u % 3, 0:nk], psum[3 + u % 3][:, 0:nk], ACT.Exp, scale=-1.0,
                                      bias=neg_m[:, pr, x["h"]:x["h"] + 1],
                                      accum_out=row_sum[:, pr, x["h"]:x["h"] + 1]).then_inc(S["p_ready"], 1)
                        if kind == "band" and x["last"]:
                            ac.wait_ge(S["sink_arg"], x["t"] + 1)
                            ac.activation(sink_e[:, pr, :], sink_e[:, pr, :], ACT.Exp).then_inc(S["sink_exp"], 1)
                    if 2 <= i <= n + 1:
                        x = units[i - 2]
                        u = x["u"]
                        nk = len(x["blocks"]) * P
                        ac.wait_ge(S["pt_ready"], u + 1)
                        if u >= 2:
                            ac.wait_ge(S["av_done"], u - 1)
                        ac.activation(probsT[:, u % 2, 0:nk], psum[6 + u % 2][:, 0:nk], ACT.Copy).then_inc(S["pt_copied"], 1)
                        if x["last"]:
                            tile_end[i + 3] = (x["g"], x["t"])
                    if i in tile_end:
                        g, t = tile_end[i]
                        ac.wait_ge(S["ot_ready"], g + 1)
                        ac.activation(dst[:, 0:4, t * P:(t + 1) * P],
                                      psum[2][:, :].rearrange("p (a b) -> p a b", a=4), ACT.Copy).then_inc(S["ot_copied"], 1)
                assert len(tile_end) == NT

            attend("band", yaT)
            for g in range(4):
                evac(sqT[:, 4 + g, :])
            for g in range(4):
                evac(ycT[:, g, :], scale=cols[:, COLS["pool_scale"]][:, g:g + 1])
            for n in range(3):
                if n == 0:
                    ac.wait_ge(S["yb_ready"], 4)
                    ac.wait_ge(S["mem_ready"], KB)
                else:
                    ac.wait_ge(S["merged_ready"], KB * n)
                with ac.Fori(0, 2) as i:
                    loop[0] = (i, 4)
                    for s in range(4):
                        evac(gates[:, ds(i * 4 + s, 1), :].rearrange("p a b -> p (a b)"), ACT.Sigmoid)
                    loop[0] = None
                lin[0] += 4
                for k in range(KB):
                    evac(sqT[:, k, :])

            def z_evac(k):
                b = ready()
                ac.activation(sqT[:, k, :], b[:, :], ACT.Square).then_inc(S["sq_ready"], 1)
                ac.activation(zT[:, k, :], b[:, :], ACT.Copy).then_inc(S["lin_evacuated"], 1)

            def residual_norms(k):
                squares(lambda b: xT[:, b, :], KB, wait=lambda b: ac.wait_ge(S["x_ready"], KB * k + b + 1))
            ac.wait_ge(S["merged_ready"], 3 * KB)
            for k in range(KB):
                z_evac(k)
            norm_std(D)
            residual_norms(0)
            norm_std(D)
            for j in range(4):
                evac(qmT[:, j, :], scale=-1.0 / math.sqrt(128))
            attend("mem", ymT)
            for k in range(KB):
                z_evac(k)
            norm_std(D)
            residual_norms(1)
            norm_std(D)
            with ac.Fori(0, 8) as i:
                loop[0] = (i, 4)
                for s in range(4):
                    evac(hid[:, ds(i * 4 + s, 1), :].rearrange("p a b -> p (a b)"), ACT.Relu)
                loop[0] = None
            lin[0] += 28
            for k in range(KB):
                z_evac(k)
            norm_std(D)
            evac(mod_cols, width=2 * KB)
            for s in range(2, 6):
                for half in range(2):
                    evac(mod[:, s, half * 512:(half + 1) * 512])
            residual_norms(2)
            norm_std(D)
            for k in range(5):
                b = ready()
                ac.activation(sqT[:, k, :], b[:, :], ACT.Square).then_inc(S["sq_ready"], 1)
                ac.activation(cqT[:, k, :], b[:, :], ACT.Copy).then_inc(S["lin_evacuated"], 1)
            for t in range(NT):
                evac(misc_tok[:, t, :], width=40)

            def tok(dst):
                for t in range(NT):
                    evac(dst[:, t, :])

            def tok_squares(n, src, width):
                if n >= 1:
                    ac.wait_ge(S["tok_ss"], n)
                flat = src.rearrange("p t n -> p (t n)") if n < 2 else src.rearrange("p t h d -> p (t h d)")
                ac.activation(sq_tok.rearrange("p t n -> p (t n)")[:, 0:NT * HEADS * width], flat, ACT.Square)\
                  .then_inc(S["tok_std"], 1)

            def tok_std(n, width):
                ac.wait_ge(S["tok_ss"], n + 1)
                ac.activation(r_tok, ss_tok, ACT.Sqrt, scale=1.0 / width, bias=eps[:, 0:1]).then_inc(S["tok_std"], 1)
            tok(fq_tok)
            norm_std(384)
            norm_std(256)
            tok(fk_tok)
            ac.wait_ge(S["fl_arg"], 1)
            ac.activation(fl_b, fl_b, ACT.Exp, scale=-1.0).then_inc(S["fl_exp"], 1)
            ac.wait_ge(S["fl_exp"], 1)
            ac.activation(fl_b, fl_b, ACT.Ln, bias=ones[:, 0:1]).then_inc(S["fl_exp"], 1)
            ac.wait_ge(S["lin_evacuated"], lin[0])
            tok_squares(0, fq_tok, 64)
            tok_std(0, 64)
            tok_squares(1, fk_tok, 64)
            tok(v_fox)
            tok_std(1, 64)
            ac.wait_ge(S["trig_arg"], 1)
            ac.activation(sin_t, sin_t, ACT.Sin).then_inc(S["trig_ready"], 1)
            ac.activation(cos_t, cos_t, ACT.Sin).then_inc(S["trig_ready"], 1)
            for t in range(NT):
                evac(k_tok[:, t, :, 0:64], src=lambda b: b[:, :].rearrange("p (h d) -> p h d", h=HEADS))
            tok(v_mla)
            ac.wait_ge(S["tok_sq"], 1)
            ac.wait_ge(S["lin_evacuated"], lin[0])
            tok_squares(2, k_tok, QK)
            tok_std(2, QK)
            for half in range(2):
                for t in range(NT):
                    evac(q_tok[:, t, :, :].rearrange("p h d -> p (h d)")[:, half * 384:(half + 1) * 384], width=384)
            evac(f_log, rows_=HEADS)
            ac.wait_ge(S["lin_evacuated"], lin[0])
            tok_squares(3, q_tok, QK)
            for dst in (fqT, fkT):
                for j in range(4):
                    evac(dst[:, j, :])
            tok_std(3, QK)
            for h in range(HEADS):
                evac(kT[0:QK, h, :], rows_=QK)
            evac(sm(548, 32), width=32)
            for h in range(HEADS):
                evac(f_row[:, h, :])
            for h in range(HEADS):
                evac(qT[0:QK, h, :], rows_=QK)
            attend("mla", oT[:, 0:4, :])
            attend("fox", oT[:, 4:8, :])
            for t in range(NT):
                for half in range(2):
                    evac(h2_tok[:, t, half * 512:(half + 1) * 512])
            for half in range(2):
                for t in range(NT):
                    evac(x_tok[:, t, half * 512:(half + 1) * 512])
            for t in range(NT):
                ac.wait_ge(S["x2_ready"], NT + t + 1)
                ac.activation(h2_tok[:, t, :], x_tok[:, t, :], ACT.Square, accum_out=std[:, t:t + 1]).then_inc(S["h2_sq"], 1)
                ac.wait_ge(S["h2_sq"], t + 1)
                ac.activation(rstd[:, t:t + 1], std[:, t:t + 1], ACT.Sqrt, scale=1.0 / D, bias=eps[:, 0:1]).then_inc(S["h2_std"], 1)
            for t in range(NT):
                for half in range(2):
                    b = ready()
                    ac.activation(h2T[:, half * 4:half * 4 + 4, t * P:(t + 1) * P],
                                  b[:, :].rearrange("p (a b) -> p a b", a=4), ACT.Copy).then_inc(S["lin_evacuated"], 1)

            def key_scores(n):
                if n % HEADS == 0 and n >= 2 * HEADS:
                    ac.wait_ge(S["top_arg"], n - HEADS)
                h = n % HEADS
                ac.wait_ge(S["sc_ready"], n + 1)
                ac.activation(scores[n // HEADS % 2][:, 2 * h * P:2 * (h + 1) * P], psum[4 + n % 2][:, 0:2 * P], ACT.Copy)\
                  .then_inc(S["sc_copied"], 1)

            def gate_exp(n):
                ac.wait_ge(S["top_arg"], n + 1)
                t, h = n // HEADS, n % HEADS
                g = gate_w[:, t % 2, h * TOPK:(h + 1) * TOPK]
                ac.activation(g, g, ACT.Exp, accum_out=gsum[:, n % 2:n % 2 + 1]).then_inc(S["top_exp"], 1)

            n_groups = NT * ROWS_PER_TILE // UG
            per_tile = ROWS_PER_TILE // UG

            def group(n):
                if n < n_groups:
                    ac.wait_ge(S["u_used"], UG * (n + 1))
                    if n >= 2:
                        ac.wait_ge(S["w_ready"], n - 1)
                    ac.activation(gl[:, n % 2, :], dots[:, n % 2, :], ACT.Gelu_apprx_tanh).then_inc(S["gl_ready"], 1)
                    if n % PER_HEAD == 2 and n // PER_HEAD + 2 < NT * HEADS:
                        gate_exp(n // PER_HEAD + 2)
                m = n - AHEAD
                if m >= 0:
                    ac.wait_ge(S["w_ready"], m + 1)
                    for s in range(UG):
                        if m >= 1:
                            ac.wait_ge(S["v_used"], UG * (m - 1) + s + 1)
                        ac.activation(wdiag[:, s, :], ident, ACT.Copy, scale=wts[:, m % W_RING, s:s + 1]).then_inc(S["dg_ready"], 1)
            for h in range(HEADS):
                for p in range(2):
                    evac(qpT[:, 2 * h + p, :])
                key_scores(h)
                if h < 2:
                    gate_exp(h)
                if h >= 1:
                    group(2 * h - 2)
                    group(2 * h - 1)
            for n in range(QUERY_GROUPS, n_groups + AHEAD):
                if n % per_tile == AHEAD and n // per_tile + 1 < NT:
                    for h in range(HEADS):
                        key_scores(HEADS * (n // per_tile + 1) + h)
                group(n)

        @block.vector
        def _(ve):
            st = Steps(ve, S["dve_own"])
            norms = [0]

            def spread(n_tiles=NT):
                norms[0] += 1
                ve.wait_ge(S["std_ready"], norms[0])
                st(ve.reciprocal(rstd[:, 0:n_tiles], std[:, 0:n_tiles]))
                st(ve.tensor_tensor(diag[:, 0:n_tiles, :], ident.unsqueeze(1).to_broadcast([P, n_tiles, P]),
                                    rstd[:, 0:n_tiles].unsqueeze(2).to_broadcast([P, n_tiles, P]), ALU.mult), S["diag_ready"])
                ve.wait_ge(S["rbc_ready"], norms[0])

            def scale_blocks(dst, src, gain, nb, sem_, width=SEQ):
                for k in range(nb):
                    st(ve.scalar_tensor_tensor(dst[:, k, :], src[:, k, :], gain[:, k:k + 1], psum[7][:, 0:width],
                                               ALU.mult, ALU.mult), sem_)

            def residual(gain, evacuated):
                spread()
                ve.wait_ge(S["lin_evacuated"], evacuated)
                for k in range(KB):
                    st(ve.scalar_tensor_tensor(zT[:, k, :], zT[:, k, :], gain[:, k:k + 1], psum[7][:, :], ALU.mult, ALU.mult))
                    st(ve.tensor_tensor(xT[:, k, :], xT[:, k, :], zT[:, k, :], ALU.add), S["x_ready"])

            ve.wait_ge(S["cols_in"], 16)
            ve.wait_ge(S["consts_in"], 16)
            ve.wait_ge(S["x_in"], 16)
            spread()
            scale_blocks(hT, xT, cols[:, COLS["g0"]], KB, S["h_ready"])
            spread(2)
            scale_blocks(memT, memT, cols[:, COLS["g_mem"]], KB, S["mem_ready"], width=N_MEM)
            ve.wait_ge(S["sig_c"], 1)
            st(ve.tensor_tensor(silu_c[:, :], silu_c[:, :], cols[:, COLS["c"]], ALU.mult), S["silu_ready"])
            st(ve.memset(cT[:, :, 0:POOL_PAD], 0.0))
            st(ve.memset(pool_a[:, 0:POOL_PAD], 0.0))
            st(ve.memset(pool_b[:, 0:POOL_PAD], 0.0))
            ve.wait_ge(S["sgu_in"], 64)
            st(ve.memset(w_spT[64:P, :, 0:64], 0.0), S["wsp_ready"])
            for t in range(NT):
                ve.wait_ge(S["lin_evacuated"], t + 1)
                st(ve.tensor_tensor(sqT[:, 4 + t, :], vS[:, t, :], vS[:, t, :], ALU.mult))
                st(ve.reduce_sum(rstd[:, t:t + 1], sqT[:, 4 + t, :], axis=AX_X), S["v_sq_ready"])
            ve.wait_ge(S["vstd_ready"], 1)
            st(ve.reciprocal(rstd[:, :], std[:, :]))
            for t in range(NT):
                st(ve.scalar_tensor_tensor(vS[:, t, :], vS[:, t, :], rstd[:, t:t + 1], g_sgu_row, ALU.mult, ALU.mult), S["vs_ready"])
            for g in range(4):
                ve.wait_ge(S["lin_evacuated"], 4 + g + 1)
                src = cT[:, g, :]
                for lvl in range(g + 1):
                    dst = (pool_a, pool_b)[lvl % 2]
                    sh = 1 << lvl
                    st(ve.tensor_tensor(dst[:, POOL_PAD:], src[:, POOL_PAD:], src[:, POOL_PAD - sh:POOL_PAD - sh + SEQ], ALU.add))
                    src = dst
                st(ve.tensor_tensor(src[:, POOL_PAD:], src[:, POOL_PAD:], inv_cnt[:, g, :], ALU.mult))
                st(ve.tensor_tensor(cT[:, g, POOL_PAD:], src[:, POOL_PAD:], cT[:, g, POOL_PAD:], ALU.subtract), S["pooled_ready"])

            def attend(kind):
                units, heads = plan[kind]["units"], plan[kind]["heads"]
                dv = 512 // heads
                n = len(units)
                tile_end = {}
                for i in range(n + 5):
                    if i < n:
                        x = units[i]
                        u, h, t, pr = x["u"], x["h"], x["t"], x["g"] % 2
                        nk = len(x["blocks"]) * P
                        s = psum[3 + u % 3]
                        ve.wait_ge(S["s_ready"], u + 1)
                        low = neg_m[:, pr, h:h + 1]
                        causal = cst[:, CST["mask_causal"]][:, SEQ - nk:]
                        if kind == "band":
                            st(ve.tensor_tensor_reduce(out=s[:, 0:nk], in0=s[:, 0:nk], in1=cst[:, CST["mask_band"]][:, 256 - nk:256],
                                                       scale=1.0, scalar=3.0e38, op0=ALU.add, op1=ALU.min, accum_out=mx[:, pr, h:h + 1]))
                            st(ve.tensor_tensor(low, mx[:, pr, h:h + 1], rows[:, ROWS["sinks"]][:, h:h + 1], ALU.min), S["neg_ready"])
                        elif kind == "mem":
                            st(ve.tensor_reduce(low, s[:, 0:nk], axis=AX_X, op=ALU.min), S["neg_ready"])
                        else:
                            if kind == "fox":
                                st(ve.scalar_tensor_tensor(s[:, 0:nk], s[:, 0:nk], fq_col[:, t, h:h + 1], f_row[:, h, 0:nk],
                                                           ALU.subtract, ALU.add))
                            st(ve.tensor_tensor_reduce(out=s[:, 0:nk], in0=s[:, 0:nk], in1=causal, scale=1.0, scalar=3.0e38,
                                                       op0=ALU.add, op1=ALU.min, accum_out=low), S["neg_ready"])
                        if x["last"]:
                            tile_end[i + 4] = x
                            if kind == "band":
                                st(ve.tensor_tensor(sink_e[:, pr, :], neg_m[:, pr, :], rows[:, ROWS["sinks"]], ALU.subtract), S["sink_arg"])
                    if i in tile_end:
                        x = tile_end[i]
                        g, pr = x["g"], x["g"] % 2
                        ve.wait_ge(S["av_done"], x["u"] + 1)
                        if kind == "band":
                            ve.wait_ge(S["sink_exp"], x["t"] + 1)
                            st(ve.tensor_tensor(row_sum[:, pr, :], row_sum[:, pr, :], sink_e[:, pr, :], ALU.add))
                        st(ve.reciprocal(row_sum[:, pr, 0:heads], row_sum[:, pr, 0:heads]))
                        if g >= 2:
                            ve.wait_ge(S["ot_ready"], g - 1)
                        st(ve.tensor_tensor(o_tok[:, g % 2, :].rearrange("p (h d) -> p h d", h=heads),
                                            psum[g % 2][:, :].rearrange("p (h d) -> p h d", h=heads),
                                            row_sum[:, pr, 0:heads].unsqueeze(2).to_broadcast([P, heads, dv]), ALU.mult), S["o_normed"])
                assert len(tile_end) == NT

            ve.wait_ge(S["rows_in"], 16)
            st(ve.tensor_scalar(rows[:, ROWS["sinks"]], rows[:, ROWS["sinks"]], -1.0, None, ALU.mult))
            attend("band")
            for g in range(4):
                ve.wait_ge(S["lin_evacuated"], 27 + g + 1)
                sp = sqT[:, 4 + g, :].rearrange("p (t i) -> p t i", t=NT)
                st(ve.tensor_tensor(sp, sp, b_sp_row[:, g, :].unsqueeze(1).to_broadcast([P, NT, P]), ALU.add))
                st(ve.tensor_tensor(uT[:, g, :], uT[:, g, :], sqT[:, 4 + g, :], ALU.mult), S["yb_ready"])
            base = 35
            for n in range(3):
                for k in range(KB):
                    ve.wait_ge(S["lin_evacuated"], base + 16 * n + KB + k + 1)
                    if n == 0:
                        st(ve.tensor_tensor(merged[:, k, :], gates[:, k, :], sqT[:, k, :], ALU.mult), S["merged_ready"])
                    else:
                        st(ve.tensor_tensor(sqT[:, k, :], gates[:, k, :], sqT[:, k, :], ALU.mult))
                        st(ve.tensor_tensor(merged[:, k, :], merged[:, k, :], sqT[:, k, :], ALU.add), S["merged_ready"])
            base += 48 + KB
            residual(cols[:, COLS["g1"]], base)
            spread()
            scale_blocks(hT, xT, cols[:, COLS["g2"]], KB, S["h_ready"])
            base += 4
            attend("mem")
            base += KB
            residual(cols[:, COLS["g3"]], base)
            spread()
            scale_blocks(hT, xT, cols[:, COLS["g4"]], KB, S["h_ready"])
            ve.wait_ge(S["ada_b_in"], 16)
            with ve.Fori(0, 8) as i:
                st.enter(i, ((S["dve_own"], 1), (S["hid_ready"], 4), (S["ada_used"], 6)))
                st(ve.tensor_copy(c_now[:, :], silu_c[:, ds(i, 1)]))
                for s in range(6):
                    if s >= 2:
                        ve.wait_ge(S["lin_evacuated"], i * 4 + (base + s - 1))
                        h_ = hid[:, ds(i * 4 + (s - 2), 1), :].rearrange("p a b -> p (a b)")
                        st(ve.tensor_tensor(h_, h_, h_, ALU.mult), S["hid_ready"])
                    ve.wait_ge(ada_landed[s % 2], i * 48 + 16 * (s // 2 + 1))
                    st(ve.scalar_tensor_tensor(mod[:, s, :], ada_ring[:, s % 2, :], c_now[:, 0:1], mod[:, s, :],
                                               ALU.mult, ALU.add), S["ada_used"])
            st.leave(8)
            base += 32 + KB
            residual(cols[:, COLS["g5"]], base)
            base += 9
            ve.wait_ge(S["lin_evacuated"], base - 8)
            st(ve.scalar_tensor_tensor(mod_cols[:, KB:], mod_cols[:, KB:], 1.0, cols[:, COLS["norm1_g"]], ALU.add, ALU.mult))
            spread()
            for k in range(KB):
                st(ve.scalar_tensor_tensor(hT[:, k, :], xT[:, k, :], mod_cols[:, KB + k:KB + k + 1], psum[7][:, :], ALU.mult, ALU.mult))
                st(ve.tensor_scalar(hT[:, k, :], hT[:, k, :], mod_cols[:, k:k + 1], None, ALU.add), S["h_ready"])
            ve.wait_ge(S["pos_in"], 16)
            st(ve.tensor_copy(pos_f, pos_i[:, :]))
            a3 = ang.rearrange("p (t n) -> p t n", t=NT)
            st(ve.tensor_tensor(a3, pos_f.unsqueeze(2).to_broadcast([P, NT, ROPE_HALF]),
                                cst[:, CST["inv_freq"]].unsqueeze(1).to_broadcast([P, NT, ROPE_HALF]), ALU.mult))
            st(ve.tensor_scalar(turns, ang, 1.0 / (2 * math.pi), MAGIC, ALU.mult, ALU.add))
            st(ve.tensor_scalar(turns, turns, -MAGIC, None, ALU.add))
            for part in (TWO_PI_A, TWO_PI_B, TWO_PI_C):
                st(ve.scalar_tensor_tensor(ang, turns, -part, ang, ALU.mult, ALU.add))
            lim = 3.1415925
            st(ve.tensor_scalar(sin_t, ang, lim, -lim, ALU.min, ALU.max))
            st(ve.tensor_scalar(cos_t, ang, math.pi / 2, None, ALU.add))
            st(ve.tensor_scalar(turns, cos_t, math.pi, -2 * math.pi, ALU.is_gt, ALU.mult))
            st(ve.tensor_tensor(cos_t, cos_t, turns, ALU.add))
            st(ve.tensor_scalar(cos_t, cos_t, lim, -lim, ALU.min, ALU.max), S["trig_arg"])
            st(ve.tensor_scalar(rows[:, ROWS["fox_q_g"]], rows[:, ROWS["fox_q_g"]], -0.125, None, ALU.mult))
            st(ve.tensor_scalar(rows[:, ROWS["mla_q_g"]], rows[:, ROWS["mla_q_g"]], -QK ** -0.5, None, ALU.mult))
            spread()
            ve.wait_ge(S["lin_evacuated"], base + 5)
            for k in range(3):
                st(ve.scalar_tensor_tensor(cqT[:, k, :], cqT[:, k, :], cols[:, COLS["qa_g"]][:, k:k + 1], psum[7][:, :],
                                           ALU.mult, ALU.mult), S["cqn_ready"])
            spread()
            for k in range(2):
                st(ve.scalar_tensor_tensor(cqT[:, 3 + k, :], cqT[:, 3 + k, :], cols[:, COLS["kva_g"]][:, k:k + 1], psum[7][:, :],
                                           ALU.mult, ALU.mult), S["cqn_ready"])
            base += 5 + 4 + 12
            z3 = fl_a.rearrange("p (t h) -> p t h", t=NT)
            st(ve.tensor_tensor(z3, misc_tok[:, :, 32:40], rows[:, ROWS["b_f"]].unsqueeze(1).to_broadcast([P, NT, HEADS]), ALU.add))
            st(ve.tensor_scalar(fl_b, fl_a, -1.0, None, ALU.mult))
            st(ve.tensor_tensor(fl_b, fl_b, fl_a, ALU.max), S["fl_arg"])
            for t in range(NT):
                st(ve.tensor_copy(k_tok[:, t, :, 64:QK], misc_tok[:, t, 0:32].unsqueeze(1).to_broadcast([P, HEADS, 32])),
                   S["tok_sq"] if t == NT - 1 else None)
            ve.wait_ge(S["fl_exp"], 2)
            st(ve.scalar_tensor_tensor(fl_a, fl_a, 0.0, fl_b, ALU.min, ALU.subtract), S["fl_ready"])
            base += 17

            def head_norm(n, src, gain, dd):
                flat = src.rearrange("p t n -> p (t n)") if n < 2 else src.rearrange("p t h d -> p (t h d)")
                v = flat.rearrange("p (a d) -> p a d", d=dd)
                ve.wait_ge(S["tok_std"], 2 * n + 1)
                st(ve.reduce_sum(ss_tok, sq_tok.rearrange("p t n -> p (t n)")[:, 0:32 * dd].rearrange("p (a d) -> p a d", d=dd), axis=AX_X),
                   S["tok_ss"])
                ve.wait_ge(S["tok_std"], 2 * n + 2)
                st(ve.reciprocal(r_tok, r_tok))
                st(ve.tensor_tensor(v, v, r_tok.unsqueeze(2).to_broadcast([P, 32, dd]), ALU.mult))
                st(ve.tensor_tensor(v, v, rows[:, ROWS[gain]].unsqueeze(1).to_broadcast([P, 32, dd]), ALU.mult),
                   S["tok_ready"] if n < 2 else None)

            def rotate(src):
                x1, x2 = src[:, :, :, 64:80], src[:, :, :, 80:96]
                tm = [rope_tmp[:, q * 512:(q + 1) * 512].rearrange("p (t h d) -> p t h d", t=NT, h=HEADS) for q in range(2)]

                def times(dst, a, trig):
                    for t in range(NT):
                        tr = trig.rearrange("p (t d) -> p t d", t=NT)[:, t, :].unsqueeze(1).to_broadcast([P, HEADS, ROPE_HALF])
                        st(ve.tensor_tensor(dst[:, t, :, :], a[:, t, :, :], tr, ALU.mult))
                times(tm[0], x1, cos_t)
                times(tm[1], x2, sin_t)
                st(ve.tensor_tensor(tm[0], tm[0], tm[1], ALU.subtract))
                times(tm[1], x1, sin_t)
                times(x2, x2, cos_t)
                st(ve.tensor_tensor(x2, x2, tm[1], ALU.add))
                st(ve.tensor_copy(x1, tm[0]), S["tok_ready"])
            head_norm(0, fq_tok, "fox_q_g", 64)
            head_norm(1, fk_tok, "fox_k_g", 64)
            ve.wait_ge(S["trig_ready"], 2)
            head_norm(2, k_tok, "mla_k_g", QK)
            rotate(k_tok)
            ve.wait_ge(S["lin_evacuated"], base)
            st(ve.tensor_tensor_scan(f_cum, ones[0:HEADS, 0:1].to_broadcast([HEADS, SEQ]), f_log, 0.0, ALU.mult, ALU.add), S["f_cum_ready"])
            head_norm(3, q_tok, "mla_q_g", QK)
            rotate(q_tok)
            base += 9
            base += 24
            attend("mla")
            attend("fox")
            ve.wait_ge(S["gn2_in"], 16)
            st(ve.scalar_tensor_tensor(mod[:, 4, :], mod[:, 4, :], 1.0, mod[:, 0, :], ALU.add, ALU.mult))
            base += 8
            for half in range(2):
                hs = slice(half * 512, (half + 1) * 512)
                for t in range(NT):
                    ve.wait_ge(S["lin_evacuated"], base + half * NT + t + 1)
                    st(ve.tensor_tensor(x_tok[:, t, hs], x_tok[:, t, hs], mod[:, 2, hs], ALU.mult))
                    st(ve.tensor_tensor(x_tok[:, t, hs], x_tok[:, t, hs], h2_tok[:, t, hs], ALU.add), S["x2_ready"])
            for t in range(NT):
                ve.wait_ge(S["h2_std"], t + 1)
                st(ve.reciprocal(rstd[:, t:t + 1], rstd[:, t:t + 1]))
                st(ve.scalar_tensor_tensor(h2_tok[:, t, :], x_tok[:, t, :], rstd[:, t:t + 1], mod[:, 4, :], ALU.mult, ALU.mult))
                st(ve.tensor_tensor(h2_tok[:, t, :], h2_tok[:, t, :], mod[:, 3, :], ALU.add), S["h2_ready"])

            def top16(vals, n, v_out, i_out):
                st(ve.max(v_out[:, 0:8], vals))
                st(ve.max_index(i_out[:, 0:8], v_out[:, 0:8], vals))
                st(ve.match_replace(vals, v_out[:, 0:8], vals, -3.0e38))
                st(ve.max(v_out[:, 8:16], vals))
                st(ve.max_index(i_out[:, 8:16], v_out[:, 8:16], vals))

            def route(n):
                t, h = n // HEADS, n % HEADS
                ve.wait_ge(S["sc_copied"], n + 1)
                for p in range(2):
                    k = 2 * h + p
                    top16(scores[t % 2][:, k * P:(k + 1) * P], P, top_v[:, p * TOPK:(p + 1) * TOPK], top_i[:, p * TOPK:(p + 1) * TOPK])
                st(ve.tensor_copy(top_if[:, :], top_i[:, :]))
                c3 = cand.rearrange("p (i j) -> p i j", i=TOPK)
                st(ve.tensor_tensor(c3, top_v[:, 0:TOPK].unsqueeze(2).to_broadcast([P, TOPK, TOPK]),
                                    top_v[:, TOPK:].unsqueeze(1).to_broadcast([P, TOPK, TOPK]), ALU.add))
                top16(cand, 256, best_v[:, :], best_i[:, :])
                st(ve.tensor_scalar(best_hi[:, 0:TOPK], best_i[:, :], 4, None, ALU.logical_shift_right))
                st(ve.tensor_scalar(best_hi[:, TOPK:], best_i[:, :], 15, None, ALU.bitwise_and))
                st(ve.tensor_copy(best_f[:, :], best_hi[:, :]))
                oh = onehot[:, :].rearrange("p (k i) -> p k i", i=TOPK)
                st(ve.tensor_tensor(oh, best_f[:, :].unsqueeze(2).to_broadcast([P, 2 * TOPK, TOPK]),
                                    cst[:, CST["iota16"]].unsqueeze(1).to_broadcast([P, 2 * TOPK, TOPK]), ALU.is_equal))
                for p in range(2):
                    o = oh[:, p * TOPK:(p + 1) * TOPK, :]
                    st(ve.tensor_tensor(o, o, top_if[:, p * TOPK:(p + 1) * TOPK].unsqueeze(1).to_broadcast([P, TOPK, TOPK]), ALU.mult))
                st(ve.reduce_sum(e_f[:, :], oh, axis=AX_X))
                st(ve.scalar_tensor_tensor(e_f[:, 0:TOPK], e_f[:, 0:TOPK], float(N_KEYS), e_f[:, TOPK:], ALU.mult, ALU.add))
                st(ve.tensor_copy(idx[:, t, h * TOPK:(h + 1) * TOPK], e_f[:, 0:TOPK]))
                st(ve.tensor_scalar(gate_w[:, t % 2, h * TOPK:(h + 1) * TOPK], best_v[:, :], best_v[:, 0:1], None, ALU.subtract), S["top_arg"])
                ve.wait_ge(S["top_exp"], n + 1)
                st(ve.reciprocal(gsum[:, n % 2:n % 2 + 1], gsum[:, n % 2:n % 2 + 1]))
                g = gate_w[:, t % 2, h * TOPK:(h + 1) * TOPK]
                st(ve.tensor_scalar(g, g, gsum[:, n % 2:n % 2 + 1], None, ALU.mult))

            route(0)
            route(1)
            per_tile = ROWS_PER_TILE // UG

            def weigh(n):
                t, q = n // per_tile, n % per_tile
                ve.wait_ge(S["gl_ready"], n + 1)
                if n >= W_RING:
                    ve.wait_ge(S["dg_ready"], UG * (n - W_RING + 1))
                st(ve.tensor_tensor(wts[:, n % W_RING, :], gl[:, n % 2, :], gate_w[:, t % 2, q * UG:(q + 1) * UG], ALU.mult), S["w_ready"])

            def finish(t):
                ve.wait_ge(S["v_used"], ROWS_PER_TILE * (t + 1))
                for half in range(2):
                    hs = slice(half * 512, (half + 1) * 512)
                    st(ve.tensor_tensor(h2_tok[:, t, hs], psum[(6, 0)[t % 2] + half][:, :], mod[:, 5, hs], ALU.mult))
                    st(ve.tensor_tensor(x_tok[:, t, hs], x_tok[:, t, hs], h2_tok[:, t, hs], ALU.add),
                       S["y_added"] if half else None)
            for t in range(NT):
                for q in range(per_tile):
                    n = t * per_tile + q
                    for s in range(UG):
                        slot = n % 2 * UG + s
                        ve.wait_ge(u_landed[slot], 16 * (n // 2 + 1))
                        if n >= 2 and s == 0:
                            ve.wait_ge(S["gl_ready"], n - 1)
                        st(ve.tensor_tensor_reduce(out=u_rows[:, slot, :], in0=u_rows[:, slot, :], in1=h2_tok[:, t, :], scale=1.0,
                                                   scalar=0.0, op0=ALU.mult, op1=ALU.add, accum_out=dots[:, n % 2, s:s + 1]), S["u_used"])
                    if n >= 1:
                        weigh(n - 1)
                    if n % PER_HEAD == 2 and n // PER_HEAD + 2 < NT * HEADS:
                        route(n // PER_HEAD + 2)
                    if t >= 1 and q == AHEAD + 6:
                        finish(t - 1)
            weigh(NT * per_tile - 1)
            finish(NT - 1)


def _chunks_fm(w, kb=KB):
    K, N = w.shape
    blocks = w.reshape(K // P, P, N // P, P).transpose(2, 1, 0, 3)
    blocks = blocks.reshape(N // P, P, K)
    if K <= CH:
        m = CH // K
        return blocks.reshape(N // P // m, m, P, K).transpose(0, 2, 1, 3).reshape(-1, P, CH)
    return blocks.reshape(N // P, P, K // CH, CH).transpose(0, 2, 1, 3).reshape(-1, P, CH)


def _chunks_tok(w, pad=0):
    K, N = w.shape
    per = CH // N
    if pad:
        a = w.reshape(K // P, P, N).transpose(1, 0, 2).reshape(1, P, K // P * N)
        return np.concatenate([a, np.zeros((1, P, CH - a.shape[2]), w.dtype)], axis=2)
    if N * (K // P) < CH or CH % N:
        a = w.reshape(K // P, P, N)
        return np.concatenate([a, np.zeros((K // P, P, CH - N), w.dtype)], axis=2) if N < CH else a
    return w.reshape(K // P // per, per, P, N).transpose(0, 2, 1, 3).reshape(-1, P, CH)


def lay_out(i):
    g = lambda n: np.asarray(i[n])
    x, w_in, w_in2 = g("x")[0], g("w_in")[0], g("w_in_2")
    col = lambda v: v.reshape(-1, P).T
    fm = lambda a: a.T.reshape(-1, P, a.shape[0]).transpose(1, 0, 2)
    q_cols = w_in[:, 0:512].reshape(D, 2, 4, 64).transpose(0, 2, 1, 3).reshape(D, 512)
    wkv = g("w_kv_mem")[0]
    gate = w_in[:, 2304:].reshape(D, 3, D)
    br = g("w_branch")[0]
    ukv = g("w_ukv_2").reshape(256, HEADS, 2, 64).transpose(0, 2, 1, 3).reshape(256, 1024)
    parts = [
        _chunks_tok(w_in[:, 1280:1792]), _chunks_fm(w_in[:, 1792:2304]), _chunks_fm(w_in[:, 768:1280]),
        _chunks_fm(wkv[:, 0:512]), _chunks_tok(wkv[:, 512:1024]),
        _chunks_tok(w_in[:, 640:768]), _chunks_fm(q_cols), _chunks_fm(w_in[:, 512:640])]
    for n in range(3):
        parts += [_chunks_fm(gate[:, n, :]), _chunks_fm(br[n])]
    parts += [_chunks_fm(g("w_out")[0]), _chunks_fm(g("w_q_mem")[0]), _chunks_fm(g("w_o_mem")[0]),
              _chunks_fm(g("w_up")[0]), _chunks_fm(g("w_down")[0]),
              _chunks_fm(w_in2[:, 0:640]),
              _chunks_tok(np.concatenate([w_in2[:, 640:672], w_in2[:, 2208:2216]], axis=1), pad=1),
              _chunks_tok(w_in2[:, 672:1184]), _chunks_tok(w_in2[:, 1184:1696]), _chunks_tok(w_in2[:, 1696:2208]),
              _chunks_tok(ukv), _chunks_tok(g("w_uq_2")),
              _chunks_tok(g("w_o_2")[:, 0:512]), _chunks_tok(g("w_o_2")[:, 512:1024]), _chunks_fm(g("w_pq_2"))]
    counts = [p.shape[0] for p in parts]
    want = [n for _, n in STREAM[:-2]] + [4, 4, 16]
    assert counts == want, (counts, want)
    gn = g("g_norm")[0]
    cols = np.concatenate([col(g("c_2")[0])] + [col(gn[k]) for k in range(6)] +
                          [col(g("g_mem")[0]), col(g("pool_scale")[0]), col(g("mla_qa_g_2")), col(g("mla_kva_g_2")),
                           col(g("norm1_g_2"))], axis=1)
    rows = np.concatenate([g("attn_sinks")[0], g("b_f_2"), g("mla_q_g_2"), g("mla_k_g_2"), g("fox_q_g_2"), g("fox_k_g_2")])[None]
    r, c = np.arange(P)[:, None], np.arange(256)[None]
    qc, kc = r // 64 + 2, c // 64
    band = np.where((kc <= qc) & (kc >= qc - 2), 0.0, FAR)
    causal = np.where(np.arange(SEQ)[None] <= r + SEQ - P, 0.0, FAR)
    inv_freq = (np.float32(10000.0) ** (-np.arange(0, 32, 2, dtype=np.float32) / np.float32(32))).astype(np.float32)
    cst = np.concatenate([np.eye(P), band, causal, np.tile(np.arange(16), (P, 1)), np.tile(inv_freq, (P, 1))], axis=1).astype(np.float32)
    t = np.arange(SEQ)
    inv_cnt = np.concatenate([1.0 / np.minimum(t + 1, w) for w in (2, 4, 8, 16)]).astype(np.float32)[None]
    sel = np.repeat(np.eye(HEADS), P, axis=1).astype(np.float32)
    c_ = np.ascontiguousarray
    return {
        "w_stream": c_(np.concatenate(parts, axis=0)), "xT": c_(fm(x)), "memT": c_(fm(g("mem")[0])), "cols": c_(cols),
        "rows": c_(rows), "cst": c_(cst), "inv_cnt": c_(inv_cnt), "sel": c_(sel),
        "sgu_rows": c_(np.concatenate([g("g_sgu")[0], g("b_spatial")[0].reshape(-1)])[None]),
        "w_pool": c_(g("w_pool")[0].transpose(1, 0, 2)), "w_spT": c_(g("w_spatial")[0].transpose(2, 0, 1)),
        "positions": c_(g("positions_2")[0].reshape(NT, P).T), "b_ada": c_(g("b_ada_2")[None]), "w_ada": c_(g("w_ada_2")),
        "norm2_g": c_(g("norm2_g_2")[None]),
        "sub_keys": c_(g("sub_keys_2").reshape(2 * HEADS, N_KEYS, P).transpose(2, 0, 1)),
        "peer_u": c_(g("peer_u_2")), "peer_v": c_(g("peer_v_2")),
    }


def kernel(**inputs):
    import concourse.bacc as bacc
    from concourse.bass_utils import run_bass_kernel_spmd

    nc = bacc.Bacc("TRN2", target_bir_lowering=False, num_devices=1)
    arrays = lay_out(inputs)
    T = {n: nc.dram_tensor("in_" + n, a.shape, mybir.dt.from_np(a.dtype), kind="ExternalInput").ap() for n, a in arrays.items()}
    out = nc.dram_tensor("out", (SEQ, D), F32, kind="ExternalOutput").ap()
    build(nc, T, out)
    r = run_bass_kernel_spmd(nc, [{"in_" + n: a for n, a in arrays.items()}], core_ids=[0])
    return np.asarray(r.results[0]["out"]).reshape(1, SEQ, D)
```
